# Optimizing a Trainium2 kernel written in Bass

```python
import math
import jax, jax.numpy as jnp
from jax import lax
import numpy as np

D_MODEL = 1024
BATCH = 1
SEQ = 256
DEPTH = 2

GRID_W = 64
CTX_LEN = 256
HEAD_DIM = 64
ROPE_THETA = 10000.0
Q_BLOCK = 128
EPS = 1e-6
A_HEADS = D_MODEL // (2 * HEAD_DIM)
A_KV_HEADS = 2
A_GROUP = A_HEADS // A_KV_HEADS
B_HEADS = D_MODEL // (4 * HEAD_DIM)
AB_SPLITS = (A_HEADS * HEAD_DIM, A_KV_HEADS * HEAD_DIM, A_KV_HEADS * HEAD_DIM,
             B_HEADS * 2 * HEAD_DIM, B_HEADS * 2 * HEAD_DIM, B_HEADS * 2 * HEAD_DIM)
AB_IN = sum(AB_SPLITS)
AB_OUT = A_HEADS * HEAD_DIM + B_HEADS * 2 * HEAD_DIM
C_HEADS = D_MODEL // HEAD_DIM
NA_ROWS = 8
NA_COLS = 16
PEER_HEADS = 8
PEER_N_KEYS = 128
PEER_N_EXPERTS = PEER_N_KEYS * PEER_N_KEYS
PEER_TOPK = 16
PEER_QDIM = 256
PEER_CHUNK = 128

kernel_name = "hybrid_diffusion_gqa_diffattn_natten_peer"

def rms_norm(x, g):
    xf = x.astype(jnp.float32)
    y = xf * lax.rsqrt(jnp.mean(xf * xf, axis=-1, keepdims=True) + EPS)
    return (y * g.astype(jnp.float32)).astype(x.dtype)

def axial_rope_tables(n_tokens):
    t = jnp.arange(n_tokens)
    row = (t // GRID_W).astype(jnp.float32)
    col = (t % GRID_W).astype(jnp.float32)
    axis_dim = HEAD_DIM // 2
    freqs = 1.0 / (ROPE_THETA ** (jnp.arange(0, axis_dim, 2, dtype=jnp.float32) / axis_dim))
    ang = jnp.concatenate([row[:, None] * freqs, col[:, None] * freqs], axis=-1)
    return jnp.cos(ang), jnp.sin(ang)

def apply_axial_rope(x, cos, sin):
    B, S, H, D = x.shape
    xp = x.astype(jnp.float32).reshape(B, S, H, 2, 2, D // 4)
    c = cos.reshape(S, 1, 2, D // 4)
    s = sin.reshape(S, 1, 2, D // 4)
    x1 = xp[..., 0, :]
    x2 = xp[..., 1, :]
    out = jnp.stack([x1 * c - x2 * s, x1 * s + x2 * c], axis=-2)
    return out.reshape(B, S, H, D).astype(x.dtype)

def map_query_blocks(fn, qs):
    B, S = qs[0].shape[:2]
    nb = S // Q_BLOCK
    blocks = tuple(jnp.moveaxis(q.reshape((B, nb, Q_BLOCK) + q.shape[2:]), 1, 0) for q in qs)
    outs = lax.map(fn, blocks)
    return tuple(jnp.moveaxis(o, 0, 1).reshape((B, S) + o.shape[3:]) for o in outs)

def gqa_attend(q, k, v):
    s = jnp.einsum('bqhgd,bkhd->bhgqk', q, k) * (HEAD_DIM ** -0.5)
    p = jax.nn.softmax(s.astype(jnp.float32), axis=-1).astype(v.dtype)
    return jnp.einsum('bhgqk,bkhd->bqhgd', p, v)

def diff_attend(q, k, v, lam):
    s = jnp.einsum('bqhcd,bkhcd->bchqk', q, k) * (HEAD_DIM ** -0.5)
    p = jax.nn.softmax(s.astype(jnp.float32), axis=-1)
    p = (p[:, 0] - lam * p[:, 1]).astype(v.dtype)
    return jnp.einsum('bhqk,bkhe->bqhe', p, v)

def mixer_ab(h_lat, h_ctx, w_in, w_out, a_qn, a_kn, b_qn, b_kn, b_lam, b_subln, lam_init, cos, sin, need_ctx_out):
    def project(h, rope):
        B, L = h.shape[:2]
        qa, ka, va, qb, kb, vb = jnp.split(h @ w_in, np.cumsum(AB_SPLITS)[:-1].tolist(), axis=-1)
        qa = rms_norm(qa.reshape(B, L, A_HEADS, HEAD_DIM), a_qn)
        ka = rms_norm(ka.reshape(B, L, A_KV_HEADS, HEAD_DIM), a_kn)
        va = va.reshape(B, L, A_KV_HEADS, HEAD_DIM)
        qb = rms_norm(qb.reshape(B, L, 2 * B_HEADS, HEAD_DIM), b_qn)
        kb = rms_norm(kb.reshape(B, L, 2 * B_HEADS, HEAD_DIM), b_kn)
        vb = vb.reshape(B, L, B_HEADS, 2 * HEAD_DIM)
        if rope:
            qa, ka = apply_axial_rope(qa, cos, sin), apply_axial_rope(ka, cos, sin)
            qb, kb = apply_axial_rope(qb, cos, sin), apply_axial_rope(kb, cos, sin)
        qa = qa.reshape(B, L, A_KV_HEADS, A_GROUP, HEAD_DIM)
        qb = qb.reshape(B, L, B_HEADS, 2, HEAD_DIM)
        kb = kb.reshape(B, L, B_HEADS, 2, HEAD_DIM)
        return qa, ka, va, qb, kb, vb

    lf = b_lam.astype(jnp.float32)
    lam = jnp.exp(jnp.sum(lf[0] * lf[1])) - jnp.exp(jnp.sum(lf[2] * lf[3])) + lam_init

    qa_l, ka_l, va_l, qb_l, kb_l, vb_l = project(h_lat, True)
    qa_c, ka_c, va_c, qb_c, kb_c, vb_c = project(h_ctx, False)
    ka_all = jnp.concatenate([ka_c, ka_l], axis=1)
    va_all = jnp.concatenate([va_c, va_l], axis=1)
    kb_all = jnp.concatenate([kb_c, kb_l], axis=1)
    vb_all = jnp.concatenate([vb_c, vb_l], axis=1)

    def block(qs):
        qa_blk, qb_blk = qs
        return gqa_attend(qa_blk, ka_all, va_all), diff_attend(qb_blk, kb_all, vb_all, lam)

    def merge(oa, ob):
        B, L = oa.shape[:2]
        ob = rms_norm(ob, b_subln) * (1.0 - lam_init)
        o = jnp.concatenate([oa.reshape(B, L, -1), ob.reshape(B, L, -1)], axis=-1)
        return o @ w_out

    oa_l, ob_l = map_query_blocks(block, (qa_l, qb_l))
    o_lat = merge(oa_l, ob_l)
    o_ctx = None
    if need_ctx_out:
        o_ctx = merge(gqa_attend(qa_c, ka_c, va_c), diff_attend(qb_c, kb_c, vb_c, lam))
    return o_lat, o_ctx

def mixer_c(h_lat, h_ctx, w_in, w_out, qn, kn, rpb, need_ctx_out):
    def project(h):
        B, L = h.shape[:2]
        q, k, v = jnp.split(h @ w_in, 3, axis=-1)
        q = rms_norm(q.reshape(B, L, C_HEADS, HEAD_DIM), qn)
        k = rms_norm(k.reshape(B, L, C_HEADS, HEAD_DIM), kn)
        return q, k, v.reshape(B, L, C_HEADS, HEAD_DIM)

    q, k, v = project(h_lat)
    qc, kc, vc = project(h_ctx)
    B, S = h_lat.shape[:2]
    rows = S // GRID_W
    wr = min(NA_ROWS, rows)
    scale = HEAD_DIM ** -0.5
    qg = q.reshape(B, rows, GRID_W, C_HEADS, HEAD_DIM)
    kg = k.reshape(B, rows, GRID_W, C_HEADS, HEAD_DIM)
    vg = v.reshape(B, rows, GRID_W, C_HEADS, HEAD_DIM)
    r_all = jnp.arange(rows)
    row_start = jnp.clip(r_all - wr // 2, 0, rows - wr)
    j = jnp.arange(GRID_W)
    col_start = jnp.clip(j - NA_COLS // 2, 0, GRID_W - NA_COLS)
    col_idx = col_start[:, None] + jnp.arange(NA_COLS)
    dc_idx = col_idx - j[:, None] + (NA_COLS - 1)

    def row_block(args):
        q_row, r_i, rs_i = args
        band_k = lax.dynamic_slice_in_dim(kg, rs_i, wr, axis=1)
        band_v = lax.dynamic_slice_in_dim(vg, rs_i, wr, axis=1)
        kw = band_k[:, :, col_idx]
        vw = band_v[:, :, col_idx]
        dr_idx = rs_i + jnp.arange(wr) - r_i + (NA_ROWS - 1)
        bias = jnp.transpose(rpb[:, dr_idx][:, :, dc_idx], (0, 2, 1, 3))
        s_win = jnp.einsum('bqhd,brqchd->bhqrc', q_row, kw) * scale + bias[None]
        s_win = s_win.reshape(B, C_HEADS, GRID_W, wr * NA_COLS)
        s_ctx = jnp.einsum('bqhd,bkhd->bhqk', q_row, kc) * scale
        p = jax.nn.softmax(jnp.concatenate([s_win, s_ctx], axis=-1).astype(jnp.float32), axis=-1)
        p = p.astype(v.dtype)
        p_win = p[..., :wr * NA_COLS].reshape(B, C_HEADS, GRID_W, wr, NA_COLS)
        p_ctx = p[..., wr * NA_COLS:]
        return (jnp.einsum('bhqrc,brqchd->bqhd', p_win, vw)
                + jnp.einsum('bhqk,bkhd->bqhd', p_ctx, vc))

    o = lax.map(row_block, (jnp.moveaxis(qg, 1, 0), r_all, row_start))
    o_lat = jnp.moveaxis(o, 0, 1).reshape(B, S, C_HEADS * HEAD_DIM) @ w_out
    o_ctx = None
    if need_ctx_out:
        oc = gqa_attend(qc[:, :, :, None], kc, vc)
        o_ctx = oc.reshape(B, qc.shape[1], C_HEADS * HEAD_DIM) @ w_out
    return o_lat, o_ctx

def peer_ffn(h, w_q, sub_keys, expert_u, expert_v):
    B, L, D = h.shape
    xs = h.reshape(-1, PEER_CHUNK, D)

    def chunk(xc):
        T = xc.shape[0]
        qry = (xc @ w_q).reshape(T, PEER_HEADS, 2, PEER_QDIM // 2)
        s = jnp.einsum('thpd,hpnd->thpn', qry, sub_keys).astype(jnp.float32)
        s1, i1 = lax.top_k(s[:, :, 0], PEER_TOPK)
        s2, i2 = lax.top_k(s[:, :, 1], PEER_TOPK)
        cand = (s1[..., :, None] + s2[..., None, :]).reshape(T, PEER_HEADS, PEER_TOPK * PEER_TOPK)
        cand_idx = (i1[..., :, None] * PEER_N_KEYS + i2[..., None, :]).reshape(T, PEER_HEADS, PEER_TOPK * PEER_TOPK)
        top_s, top_pos = lax.top_k(cand, PEER_TOPK)
        eidx = jnp.take_along_axis(cand_idx, top_pos, axis=-1)
        g = jax.nn.softmax(top_s, axis=-1)
        u = jnp.take(expert_u, eidx, axis=0)
        a = jax.nn.gelu(jnp.einsum('td,thkd->thk', xc, u).astype(jnp.float32))
        v = jnp.take(expert_v, eidx, axis=0)
        return jnp.einsum('thk,thkd->td', (g * a).astype(xc.dtype), v)

    return lax.map(chunk, xs).reshape(B, L, D)

def setup_inputs(seed: int = 0) -> dict:
    key = jax.random.key(seed)
    ks = jax.random.split(key, 24)
    n_even = (DEPTH + 1) // 2
    n_odd = DEPTH // 2
    f32 = jnp.float32
    nrm = lambda k, shape, s: jax.random.normal(k, shape, f32) * s
    gain = lambda k, shape: 1.0 + 0.05 * jax.random.normal(k, shape, f32)
    return {
        "x": nrm(ks[0], (BATCH, SEQ, D_MODEL), 1.0),
        "c": nrm(ks[1], (BATCH, D_MODEL), 1.0),
        "ctx": nrm(ks[2], (BATCH, CTX_LEN, D_MODEL), 1.0),
        "c_ctx": nrm(ks[3], (D_MODEL,), 1.0),
        "ada_w": nrm(ks[4], (DEPTH, D_MODEL, 6 * D_MODEL), D_MODEL ** -0.5),
        "ada_b": nrm(ks[5], (DEPTH, 6 * D_MODEL), 0.02),
        "norm_g": gain(ks[6], (DEPTH, 2, D_MODEL)),
        "ab_w_in": nrm(ks[7], (n_even, D_MODEL, AB_IN), D_MODEL ** -0.5),
        "ab_w_out": nrm(ks[8], (n_even, AB_OUT, D_MODEL), AB_OUT ** -0.5),
        "a_q_norm": gain(ks[9], (n_even, HEAD_DIM)),
        "a_k_norm": gain(ks[10], (n_even, HEAD_DIM)),
        "b_q_norm": gain(ks[11], (n_even, HEAD_DIM)),
        "b_k_norm": gain(ks[12], (n_even, HEAD_DIM)),
        "b_lambda": nrm(ks[13], (n_even, 4, HEAD_DIM), 0.1),
        "b_subln": gain(ks[14], (n_even, 2 * HEAD_DIM)),
        "c_w_in": nrm(ks[15], (n_odd, D_MODEL, 3 * C_HEADS * HEAD_DIM), D_MODEL ** -0.5),
        "c_w_out": nrm(ks[16], (n_odd, C_HEADS * HEAD_DIM, D_MODEL), (C_HEADS * HEAD_DIM) ** -0.5),
        "c_q_norm": gain(ks[17], (n_odd, HEAD_DIM)),
        "c_k_norm": gain(ks[18], (n_odd, HEAD_DIM)),
        "c_rpb": nrm(ks[19], (n_odd, C_HEADS, 2 * NA_ROWS - 1, 2 * NA_COLS - 1), 0.2),
        "peer_w_q": nrm(ks[20], (DEPTH, D_MODEL, PEER_HEADS * PEER_QDIM), D_MODEL ** -0.5),
        "peer_keys": nrm(ks[21], (DEPTH, PEER_HEADS, 2, PEER_N_KEYS, PEER_QDIM // 2), (PEER_QDIM // 2) ** -0.5),
        "peer_u": nrm(ks[22], (DEPTH, PEER_N_EXPERTS, D_MODEL), D_MODEL ** -0.5),
        "peer_v": nrm(ks[23], (DEPTH, PEER_N_EXPERTS, D_MODEL), 0.1),
    }

def reference(x, c, ctx, c_ctx, ada_w, ada_b, norm_g, ab_w_in, ab_w_out, a_q_norm, a_k_norm,
              b_q_norm, b_k_norm, b_lambda, b_subln, c_w_in, c_w_out, c_q_norm, c_k_norm, c_rpb,
              peer_w_q, peer_keys, peer_u, peer_v):
    B, S, D = x.shape
    cos, sin = axial_rope_tables(S)
    for l in range(DEPTH):
        last = l == DEPTH - 1
        m_lat = (jax.nn.silu(c) @ ada_w[l] + ada_b[l]).reshape(B, 6, 1, D)
        m_ctx = (jax.nn.silu(c_ctx) @ ada_w[l] + ada_b[l]).reshape(6, 1, D)
        h_lat = rms_norm(x, norm_g[l, 0]) * (1.0 + m_lat[:, 1]) + m_lat[:, 0]
        h_ctx = rms_norm(ctx, norm_g[l, 0]) * (1.0 + m_ctx[1]) + m_ctx[0]
        i = l // 2
        if l % 2 == 0:
            lam_init = 0.8 - 0.6 * math.exp(-0.3 * l)
            o_lat, o_ctx = mixer_ab(h_lat, h_ctx, ab_w_in[i], ab_w_out[i], a_q_norm[i], a_k_norm[i],
                                    b_q_norm[i], b_k_norm[i], b_lambda[i], b_subln[i], lam_init,
                                    cos, sin, not last)
        else:
            o_lat, o_ctx = mixer_c(h_lat, h_ctx, c_w_in[i], c_w_out[i], c_q_norm[i], c_k_norm[i],
                                   c_rpb[i], not last)
        x = x + m_lat[:, 2] * o_lat
        h_lat = rms_norm(x, norm_g[l, 1]) * (1.0 + m_lat[:, 4]) + m_lat[:, 3]
        x = x + m_lat[:, 5] * peer_ffn(h_lat, peer_w_q[l], peer_keys[l], peer_u[l], peer_v[l])
        if not last:
            ctx = ctx + m_ctx[2] * o_ctx
            h_ctx = rms_norm(ctx, norm_g[l, 1]) * (1.0 + m_ctx[4]) + m_ctx[3]
            ctx = ctx + m_ctx[5] * peer_ffn(h_ctx, peer_w_q[l], peer_keys[l], peer_u[l], peer_v[l])
    return x


_drawn_inputs = setup_inputs


def setup_inputs(seed=0):
    import zlib

    import numpy as np

    out = dict(_drawn_inputs(seed))
    spreads = {}
    factors = {'norm_g': 3.122,
     'a_q_norm': 8.0,
     'a_k_norm': 8.0,
     'b_q_norm': 8.0,
     'b_k_norm': 8.0,
     'b_lambda': 8.0,
     'b_subln': 2.734,
     'c_q_norm': 8.0,
     'c_k_norm': 8.0,
     'c_rpb': 8.0}
    for name, (base, spread) in spreads.items():
        noise = np.random.default_rng([zlib.crc32(name.encode()), seed]).standard_normal(out[name].shape)
        drawn = base * np.exp(spread * noise) if base else spread * noise
        out[name] = __import__('jax').numpy.asarray(drawn.astype(out[name].dtype))
    for name, factor in factors.items():
        out[name] = (out[name] * factor).astype(out[name].dtype)
    return out
```

```python
import math
from contextlib import ExitStack

import numpy as np

import concourse.bass as bass
from concourse import mybir

F32 = mybir.dt.float32
U32 = mybir.dt.uint32
ALU = mybir.AluOpType
ACT = mybir.ActivationFunctionType
AX_X = mybir.AxisListType.X

P = 128
D = 1024
KD = D // P
SEQ = 256
CTX_LEN = 256
LAT = SEQ // P
NCH = (SEQ + CTX_LEN) // P
LAYERS = 2
HD = 64
GRID_W = 64
EPS = 1e-6
A_HEADS, A_KV, B_HEADS = 8, 2, 4
AB_IN = 2304
A_K0, A_V0, B_Q0, B_K0, B_V0 = 512, 640, 768, 1280, 1792
C_HEADS = 16
NA_COLS = 16
HEADS, NKEYS, TOPK = 8, 128, 16
NEXP = NKEYS * NKEYS
LAM_INIT = 0.8 - 0.6 * math.exp(-0.3 * 0)
MASKED = -1.0e30
LOWEST = -3.0e38
GELU_C = math.sqrt(2.0 / math.pi)
RING = 8
DIAGS = 8
BIAS_SLOTS = 4
NEAR = 7
SKEW = 128


def constants():
    t = np.arange(SEQ)
    axis = HD // 2
    freqs = (1.0 / (10000.0 ** (np.arange(0, axis, 2, dtype=np.float32) / np.float32(axis)))).astype(np.float32)
    ang = np.stack([(t // GRID_W).astype(np.float32)[:, None] * freqs,
                    (t % GRID_W).astype(np.float32)[:, None] * freqs], 1)
    cos, sin = np.cos(ang).astype(np.float32), np.sin(ang).astype(np.float32)
    j = np.arange(GRID_W)
    start = np.clip(j - NA_COLS // 2, 0, GRID_W - NA_COLS)
    inside = (j[None] >= start[:, None]) & (j[None] < start[:, None] + NA_COLS)
    mask = np.where(inside, 0.0, MASKED).astype(np.float32)
    return {
        "ident": np.eye(P, dtype=np.float32),
        "iota": np.tile(np.arange(TOPK, dtype=np.float32), (P, 1)),
        "rope_c": np.stack([cos, cos], 2).reshape(SEQ, HD),
        "rope_s": np.stack([-sin, sin], 2).reshape(SEQ, HD),
        "win_mask": np.concatenate([mask, mask], 0),
    }


def take(eng, sem, n=1):
    eng.wait_ge(sem, n)
    eng.sem_inc(sem, -n)


class Chain:

    def __init__(self, eng, sem):
        self.eng, self.sem, self.n = eng, sem, 0

    def add(self, ins):
        ins.then_inc(self.sem, 1)
        self.n += 1

    def wait(self):
        self.eng.wait_ge(self.sem, self.n)

    def link(self, ins):
        self.add(ins)
        self.wait()

    def reset(self):
        self.wait()
        self.eng.sem_clear(self.sem)
        self.n = 0


def build(nc, a, out):
    ctx = ExitStack()
    with ctx:
        def sb(name, shape, dt=F32):
            return ctx.enter_context(nc.sbuf_tensor(name, shape, dt))

        def sem(name):
            return ctx.enter_context(nc.semaphore(name))

        xs = sb("xs", [P, NCH, D])
        mb = sb("mb", [P, 2, 3, D])
        grow = sb("grow", [P, D])
        h = sb("h", [P, NCH, D])
        o = h
        ring_w = sb("ring_w", [P, 2, KD, 512])
        hT = sb("hT", [P, KD, NCH * P])
        big = sb("big", [P, 17408])
        small = sb("small", [P, 5632])
        QKT0 = 10240
        qkT = big[:, QKT0:QKT0 + 14 * 512].rearrange("p (t n) -> p t n", t=14)
        scores = big[:, 0:NCH * 2048]
        diag = big[:, 8192:8192 + DIAGS * P].rearrange("p (s n) -> p s n", s=DIAGS)
        qryT = big[:, 9216:17408].rearrange("p (t n) -> p t n", t=16)
        y = big[:, 13312:17408].rearrange("p (c n) -> p c n", c=NCH)
        tmpA = small[:, 0:1024]
        kdup = small[:, 1024:2048].rearrange("p (c n) -> p c n", c=NCH)
        prob = small[:, 2048:3072].rearrange("p (s n) -> p s n", s=2)
        tmpB = small[:, 2048:3072]
        probT = small[:, 3072:4096].rearrange("p (s n) -> p s n", s=2)
        bias = small[:, 4096:5632].rearrange("p (s n) -> p s n", s=BIAS_SLOTS)
        pad = small[0:C_HEADS * NEAR, 3072:3072 + SKEW]
        keys = small[:, 0:2048].rearrange("p (t n) -> p t n", t=16)
        keysT = small[:, 2048:4096].rearrange("p (t n) -> p t n", t=16)
        work = small[:, 4096:4352].rearrange("p (s n) -> p s n", s=2)
        work2 = small[:, 4352:4608].rearrange("p (s n) -> p s n", s=2)
        cand = small[:, 4608:4864]
        cand2 = small[:, 4864:5120]
        onehot = small[:, 5120:5632]
        uring = [ring_w[:, s // 4, 2 * (s % 4):2 * (s % 4) + 2, :].rearrange("p a b -> p (a b)") for s in range(RING)]
        vring = [hT[:, 2 * s:2 * s + 2, :].rearrange("p a b -> p (a b)") for s in range(4)] + \
                [big[:, 9216 + 1024 * s:9216 + 1024 * (s + 1)] for s in range(4)]
        modrow = [big[0:2, QKT0:QKT0 + 6144], big[0:2, 0:6144]]
        adab = [hT[0:2].rearrange("p k n -> p (k n)"), h[0:2].rearrange("p c n -> p (c n)")]

        ident = sb("ident", [P, P])
        iota = sb("iota", [P, TOPK])
        rope_c = sb("rope_c", [P, LAT, HD])
        rope_s = sb("rope_s", [P, LAT, HD])
        win_mask = sb("win_mask", [P, GRID_W])
        gains = sb("gains", [P, 6, HD])
        subln = sb("subln", [P, 2 * HD])
        lam_in = sb("lam_in", [P, 4 * HD])
        lam2 = sb("lam2", [P, 2])
        neg_lam = sb("neg_lam", [P, 1])
        crow = sb("crow", [16, P])
        cth = sb("cth", [16, P])
        cT = sb("cT", [P, 16])
        ss = sb("ss", [P, NCH])
        rstd = sb("rstd", [P, NCH])
        hss = sb("hss", [P, NCH * 16])
        hrs = sb("hrs", [P, NCH * 16])
        negmax = sb("negmax", [P, 64])
        rsum = sb("rsum", [P, 64])
        rinv = sb("rinv", [P, 16])
        oss = sb("oss", [P, NCH * B_HEADS])
        ors = sb("ors", [P, NCH * B_HEADS])
        top = sb("top", [P, 2, TOPK])
        topi = sb("topi", [P, 2, TOPK], U32)
        topif = sb("topif", [P, 2, TOPK])
        best = sb("best", [P, 2, TOPK])
        bpos = sb("bpos", [P, TOPK], U32)
        bij = sb("bij", [P, 2, TOPK], U32)
        bijf = sb("bijf", [P, 2, TOPK])
        seli = sb("seli", [P, 2, TOPK])
        expf = sb("expf", [P, 2, TOPK])
        idxu = sb("idxu", [P, 2, TOPK], U32)
        idxv = sb("idxv", [P, 2, TOPK], U32)
        nbest = sb("nbest", [P, 2])
        gexp = sb("gexp", [P, 2, TOPK])
        gsum = sb("gsum", [P, 2])
        ginv = sb("ginv", [P, 1])
        dots = sb("dots", [P, 2, TOPK])
        gz = sb("gz", [P, TOPK])
        gz2 = sb("gz2", [P, TOPK])
        gth = sb("gth", [P, TOPK])
        coef = sb("coef", [P, 2, TOPK])
        ps = ctx.enter_context(nc.psum_tensor("ps", [P, 8, 512], F32))

        mod_dram = nc.dram_tensor("mod_scratch", [LAYERS, 2, 6 * D], F32, kind="Internal").ap()
        skew_dram = nc.dram_tensor("skew_scratch", [C_HEADS * NEAR, GRID_W, SKEW], F32, kind="Internal").ap()

        const_in = sem("const_in")
        c_in = sem("c_in")
        x_in = sem("x_in")
        adab_in = [sem(f"adab_in{n}") for n in range(LAYERS)]
        w_in = [sem(f"w_in{s}") for s in range(2)]
        mod_out = sem("mod_out")
        mod01_in = [[sem(f"mod01_in{n}_{k}") for k in range(2)] for n in range(LAYERS)]
        mod2_in = [[sem(f"mod2_in{n}_{k}") for k in range(2)] for n in range(LAYERS)]
        pad_in = sem("pad_in")
        skew_out = sem("skew_out")
        bias_in = [sem(f"bias_in{s}") for s in range(BIAS_SLOTS)]
        keys_in = [sem(f"keys_in{n}") for n in range(LAYERS)]
        u_in = [sem(f"u_in{s}") for s in range(RING)]
        v_in = [sem(f"v_in{s}") for s in range(RING)]
        out_done = sem("out_done")
        w_free = [sem(f"w_free{s}") for s in range(2)]
        bank_free = [sem(f"bank_free{b}") for b in range(8)]
        mod01_free = sem("mod01_free")
        mod2_free = sem("mod2_free")
        bias_free = sem("bias_free")
        keys_free = sem("keys_free")
        u_free = sem("u_free")
        v_free = sem("v_free")
        diag_free = sem("diag_free")
        modrow_rdy = sem("modrow_rdy")
        pad_rdy = sem("pad_rdy")
        silu_rdy = sem("silu_rdy")
        cs_rdy = sem("cs_rdy")
        cT_rdy = sem("cT_rdy")
        ada_rdy = sem("ada_rdy")
        lam_rdy = sem("lam_rdy")
        lamx_rdy = sem("lamx_rdy")
        sq_in = sem("sq_in")
        sq_rdy = sem("sq_rdy")
        ss_rdy = sem("ss_rdy")
        x_rdy = sem("x_rdy")
        h_rdy = sem("h_rdy")
        tr_rdy = sem("tr_rdy")
        hT_rdy = sem("hT_rdy")
        proj_rdy = sem("proj_rdy")
        qkv_rdy = sem("qkv_rdy")
        qk_rdy = sem("qk_rdy")
        ka_rdy = sem("ka_rdy")
        kdup_rdy = sem("kdup_rdy")
        qkT_rdy = sem("qkT_rdy")
        s_rdy = sem("s_rdy")
        max_rdy = sem("max_rdy")
        p_rdy = sem("p_rdy")
        pT_rdy = sem("pT_rdy")
        o_rdy = sem("o_rdy")
        on_rdy = sem("on_rdy")
        oT_rdy = sem("oT_rdy")
        op_rdy = sem("op_rdy")
        keysT_rdy = sem("keysT_rdy")
        qry_rdy = sem("qry_rdy")
        sc_rdy = sem("sc_rdy")
        score_rdy = sem("score_rdy")
        peer_go = sem("peer_go")
        idxu_rdy = sem("idxu_rdy")
        idxv_rdy = sem("idxv_rdy")
        best_rdy = sem("best_rdy")
        gexp_rdy = sem("gexp_rdy")
        gz_rdy = sem("gz_rdy")
        gth_rdy = sem("gth_rdy")
        coef_rdy = sem("coef_rdy")
        diag_rdy = sem("diag_rdy")
        y_rdy = sem("y_rdy")
        layer_done = sem("layer_done")
        x_out_rdy = sem("x_out_rdy")
        own_v = sem("own_v")
        own_a = sem("own_a")
        own_t = sem("own_t")

        ADA_TILES = 6 * D // 512
        chunks_out = [NCH, LAT]
        groups = [n * HEADS for n in chunks_out]
        win = [a["ab_w_in"], a["c_w_in"]]
        wout = [a["ab_w_out"], a["c_w_out"]]
        in_width = [384, 512]
        ADA_W = ADA_TILES // 2
        LAYER_W = [3 + 1 + 2, 3 + 1 + 2]

        def wbase(n, stage):
            return LAYERS * ADA_W + sum(LAYER_W[:n]) + (0, 3, 4)[stage]

        def qcol(n, c, col):
            if n == 0:
                return c * AB_IN + col
            return c * 3 * D + col if c < LAT else LAT * 3 * D + (c - LAT) * 2 * D + col - D

        def units(n):
            found = []
            if n == 0:
                for c in range(NCH):
                    for hh in range(A_HEADS):
                        found.append(dict(c=c, q=hh // 2, k=4 + hh // 4, half=hh % 2, v=A_V0 + HD * (hh // 4), w=HD,
                                          bank=0, col=hh * HD, bias=None, group=c, last=hh == A_HEADS - 1,
                                          first=hh == 0))
                for c in range(NCH):
                    for s in range(2 * B_HEADS):
                        found.append(dict(c=c, q=6 + s // 2, k=10 + s // 2, half=s % 2, v=B_V0 + 2 * HD * (s // 2),
                                          w=2 * HD, bank=s // 4, col=(s % 4) * 2 * HD, bias=None, group=NCH + c,
                                          last=s == 2 * B_HEADS - 1, first=s == 0))
            else:
                for hh in range(C_HEADS):
                    for c in range(LAT):
                        found.append(dict(c=c, q=hh // 2, k=8 + hh // 2, half=hh % 2, v=2 * D + HD * hh, w=HD,
                                          bank=c, col=(hh % 8) * HD, bias=hh, group=hh // 8,
                                          last=hh % 8 == 7 and c == 1, first=hh % 8 == 0 and c == 0))
            return found

        def kT(n, u):
            c0 = 0 if u["c"] < LAT else LAT
            rows = slice(HD * u["half"], HD * u["half"] + HD)
            if n == 0:
                return qkT[rows, u["k"], c0 * P:NCH * P], c0
            t = u["k"] - 8
            return cT_k[rows, t, :], 0

        cT_q = big[:, QKT0:QKT0 + 8 * 256].rearrange("p (t n) -> p t n", t=8)
        cT_k = big[:, QKT0 + 2048:QKT0 + 2048 + 8 * 512].rearrange("p (t n) -> p t n", t=8)

        def qT(n, u):
            rows = slice(HD * u["half"], HD * u["half"] + HD)
            cols = slice(u["c"] * P, u["c"] * P + P)
            return qkT[rows, u["q"], cols] if n == 0 else cT_q[rows, u["q"], cols]

        def spread(vec, n):
            return bass.AP(tensor=vec.tensor, offset=vec.offset, ap=[[0, P], [1, n]])

        block = ctx.enter_context(nc.Block())

        @block.sync
        def _(sp):
            sp.dma_start(crow[0:8, :], a["c"].rearrange("a (k p) -> (a k) p", p=P)).then_inc(c_in, 16)
            sp.dma_start(crow[8:16, :], a["c_ctx"].rearrange("(k p) -> k p", p=P)).then_inc(c_in, 16)
            consts = [(ident, a["ident"]), (iota, a["iota"]), (win_mask, a["win_mask"]),
                      (rope_c, a["rope_c"].rearrange("(c p) n -> p c n", p=P)),
                      (rope_s, a["rope_s"].rearrange("(c p) n -> p c n", p=P))]
            for dst, src in consts:
                sp.dma_start(dst[:], src).then_inc(const_in, 16)
            for n in range(LAYERS):
                b = a["ada_b"]
                src = bass.AP(tensor=b.tensor, offset=n * 6 * D, ap=[[0, 2], [1, 6 * D]])
                if n == 0:
                    sp.dma_start(adab[n][:, 0:2048], src[:, 0:2048]).then_inc(adab_in[n], 16)
                    sp.dma_start(adab[n][:, 2048:4096], src[:, 2048:4096]).then_inc(adab_in[n], 16)
                    sp.dma_start(small[0:2, 0:2048], src[:, 4096:6144]).then_inc(adab_in[n], 16)
                else:
                    sp.dma_start(adab[n][:, 0:4096], src[:, 0:4096]).then_inc(adab_in[n], 16)
                    sp.dma_start(small[0:2, 3072:5120], src[:, 4096:6144]).then_inc(adab_in[n], 16)

            def load_tile(slot, src, width):
                take(sp, w_free[slot])
                sp.dma_start(ring_w[:, slot, :, 0:width], src).then_inc(w_in[slot], 16)

            for n in range(LAYERS):
                src = a["ada_w"][n].rearrange("(k p) m -> p k m", p=P)
                with sp.Fori(0, ADA_TILES // 2) as i:
                    for slot in range(2):
                        load_tile(slot, src[:, :, bass.ds(i * 1024 + slot * 512, 512)], 512)
            small_in = [(gains[:, k, :], a[name][0]) for k, name in enumerate(
                ["a_q_norm", "a_k_norm", "b_q_norm", "b_k_norm", "c_q_norm", "c_k_norm"])]
            for dst, src in small_in:
                sp.dma_start(dst, spread(src, HD)).then_inc(const_in, 16)
            sp.dma_start(subln[:], spread(a["b_subln"], 2 * HD)).then_inc(const_in, 16)
            sp.dma_start(lam_in[:], spread(a["b_lambda"], 4 * HD)).then_inc(const_in, 16)
            sp.dma_start(xs[:, 0:LAT, :], a["x"][0].rearrange("(c p) n -> p c n", p=P)).then_inc(x_in, 16)
            sp.dma_start(xs[:, LAT:NCH, :], a["ctx"][0].rearrange("(c p) n -> p c n", p=P)).then_inc(x_in, 16)
            for n in range(LAYERS):
                take(sp, modrow_rdy)
                sp.dma_start(mod_dram[n], modrow[n]).then_inc(mod_out, 16)
            sp.wait_ge(mod_out, 16 * LAYERS)
            take(sp, pad_rdy)
            sp.dma_start(pad[:, 48:48 + 31], a["rpb_near"]).then_inc(pad_in, 16)
            sp.wait_ge(pad_in, 16)
            sp.dma_start(skew_dram, bass.AP(tensor=pad.tensor, offset=pad.offset,
                                            ap=[list(pad.ap[0]), [0, GRID_W], [1, SKEW]])).then_inc(skew_out, 16)

            def load_mod(n, first, rows, slot, done):
                for s in range(2):
                    src = mod_dram[n, s, first * D:(first + rows) * D]
                    sp.dma_start(mb[:, s, slot:slot + rows, :].rearrange("p r n -> p (r n)"),
                                 spread(src, rows * D)).then_inc(done, 16)

            for n in range(LAYERS):
                if n == 1:
                    take(sp, layer_done)
                sp.dma_start(grow[:], spread(a["norm_g"][n, 0], D)).then_inc(mod01_in[n][0], 16)
                load_mod(n, 0, 2, 0, mod01_in[n][0])
                load_mod(n, 2, 1, 2, mod2_in[n][0])
                wi = win[n][0].rearrange("(k p) m -> p k m", p=P)
                width = in_width[n]
                for slot in range(2):
                    load_tile(slot, wi[:, :, slot * width:(slot + 1) * width], width)
                take(sp, mod01_free)
                sp.dma_start(grow[:], spread(a["norm_g"][n, 1], D)).then_inc(mod01_in[n][1], 16)
                load_mod(n, 3, 2, 0, mod01_in[n][1])
                with sp.Fori(0, 2) as i:
                    for slot in range(2):
                        load_tile(slot, wi[:, :, bass.ds(i * (2 * width) + (2 + slot) * width, width)], width)
                wo = wout[n][0].rearrange("(k p) m -> p k m", p=P)
                for slot in range(2):
                    load_tile(slot, wo[:, :, slot * 512:(slot + 1) * 512], 512)
                if n == 1:
                    sp.wait_ge(skew_out, 16)
                    for hh in range(C_HEADS):
                        take(sp, bias_free)
                        for odd in range(2):
                            src = bass.AP(tensor=skew_dram.tensor,
                                          offset=(hh * NEAR + 1 - odd) * GRID_W * SKEW + GRID_W - 1,
                                          ap=[[SKEW - 1, GRID_W], [GRID_W * SKEW, 6], [1, GRID_W]])
                            dst = bias[GRID_W * odd:GRID_W * odd + GRID_W, hh % BIAS_SLOTS, :]
                            sp.dma_start(dst.rearrange("p (i c) -> p i c", i=6), src)\
                              .then_inc(bias_in[hh % BIAS_SLOTS], 16)
                take(sp, keys_free)
                sp.dma_start(keys, a["peer_keys"][n].rearrange("h q n d -> n (h q) d")).then_inc(keys_in[n], 16)
                wq = a["peer_w_q"][n].rearrange("(k p) m -> p k m", p=P)
                with sp.Fori(0, 2) as i:
                    for slot in range(2):
                        load_tile(slot, wq[:, :, bass.ds(i * 1024 + slot * 512, 512)], 512)
                take(sp, mod2_free)
                load_mod(n, 5, 1, 2, mod2_in[n][1])
            take(sp, x_out_rdy)
            sp.dma_start(out[0].rearrange("(c p) n -> p c n", p=P), xs[:, 0:LAT, :]).then_inc(out_done, 16)
            sp.wait_ge(out_done, 16)

        @block.gpsimd
        def _(pool):
            pool.sem_inc(u_free, RING)
            pool.sem_inc(v_free, RING)

            def gather(table, idx, ring, k, room, landed):
                take(pool, room)
                pool.indirect_dma_start(ring[k % RING], None, table,
                                        bass.IndirectOffsetOnAxis(idx[:, k:k + 1], 0)).then_inc(landed[k % RING], 16)

            def step(n, par, u, v):
                if u:
                    take(pool, idxu_rdy)
                if v:
                    take(pool, idxv_rdy)
                for k in range(TOPK):
                    if u:
                        gather(a[f"peer_u{n}"], idxu[:, par, :], uring, k, u_free, u_in)
                    if v:
                        gather(a[f"peer_v{n}"], idxv[:, 1 - par, :], vring, k, v_free, v_in)

            for n in range(LAYERS):
                take(pool, peer_go)
                step(n, 0, True, False)
                with pool.Fori(0, (groups[n] - 2) // 2):
                    step(n, 1, True, True)
                    step(n, 0, True, True)
                step(n, 1, True, True)
                step(n, 0, False, True)

        @block.scalar
        def _(act):
            bank = [0]
            own = Chain(act, own_a)

            def copy(dst, src):
                return nc.scalar.activation(dst, src, ACT.Copy)

            def tr_out(dst, width=512, shape=None):
                b = 6 + bank[0] % 2
                bank[0] += 1
                take(act, tr_rdy)
                src = ps[:, b, 0:width]
                if shape:
                    src = src.rearrange("p (t n) -> p t n", t=shape)
                copy(dst, src).then_inc(bank_free[b], 1)

            def rows_out(chunks, rdy):
                for c in range(chunks):
                    for half in range(2):
                        tr_out(hT[:, 4 * half:4 * half + 4, c * P:(c + 1) * P], shape=4)
                act.drain().then_inc(rdy, 1)

            def sumsq(chunks):
                for c in range(chunks):
                    nc.scalar.activation(h[:, c, :], xs[:, c, :], ACT.Square, accum_out=ss[:, c:c + 1])\
                      .then_inc(ss_rdy, 1)

            def root(t):
                take(act, sq_in)
                nc.scalar.activation(t, t, ACT.Sqrt).then_inc(sq_rdy, 1)

            act.wait_ge(c_in, 32)
            nc.scalar.activation(cth[:], crow[:], ACT.Tanh, scale=0.5).then_inc(silu_rdy, 1)
            take(act, lam_rdy)
            nc.scalar.activation(lam2[:], lam2[:], ACT.Exp).then_inc(lamx_rdy, 1)

            for n in range(LAYERS):
                co = chunks_out[n]
                if n == 0:
                    act.wait_ge(x_in, 32)
                    take(act, x_rdy, 1)
                else:
                    take(act, x_rdy, 1)
                sumsq(NCH)
                root(ss[:])
                rows_out(NCH, hT_rdy)
                width = in_width[n]
                first = NCH if n == 0 else LAT
                for t in range(2):
                    for c in range(first):
                        take(act, proj_rdy)
                        q0 = qcol(n, c, t * width)
                        copy(big[:, q0:q0 + width], ps[:, c, 0:width]).then_inc(bank_free[c], 1)
                act.drain().then_inc(qkv_rdy, 1)
                root(hss[:, 0:first * (10 if n == 0 else 16)])
                with act.Fori(0, 2) as i:
                    for t in range(2):
                        for c in range(NCH):
                            take(act, proj_rdy)
                            q0 = qcol(n, c, (2 + t) * width)
                            copy(big[:, bass.ds(i * (2 * width) + q0, width)], ps[:, c, 0:width])\
                                .then_inc(bank_free[c], 1)
                act.drain().then_inc(qkv_rdy, 1)
                if n == 0:
                    take(act, ka_rdy)
                    for c in range(NCH):
                        q0 = qcol(0, c, A_K0)
                        src = big[:, q0:q0 + 2 * HD]
                        src = bass.AP(tensor=src.tensor, offset=src.offset,
                                      ap=[list(src.ap[0]), [HD, 2], [0, 2], [1, HD]])
                        copy(kdup[:, c, :].rearrange("p (a b n) -> p a b n", a=2, b=2), src)
                    act.drain().then_inc(kdup_rdy, 1)
                root(hss[:, 0:NCH * 16])
                if n == 0:
                    for t in range(14):
                        tr_out(qkT[:, t, :])
                else:
                    for t in range(8):
                        tr_out(cT_q[:, t, :], width=256)
                    for t in range(8):
                        tr_out(cT_k[:, t, :])
                act.drain().then_inc(qkT_rdy, 1)
                us = units(n)

                def exp(u):
                    nk = (NCH if us[u]["c"] < LAT else NCH - LAT) * P
                    take(act, max_rdy)
                    nc.scalar.activation(prob[:, u % 2, 0:nk], ps[:, 4 + u % 2, 0:nk], ACT.Exp,
                                         bias=negmax[:, u:u + 1], accum_out=rsum[:, u:u + 1]).then_inc(p_rdy, 1)

                def pT_out(u):
                    nk = (NCH if us[u]["c"] < LAT else NCH - LAT) * P
                    take(act, tr_rdy)
                    copy(probT[:, u % 2, 0:nk], ps[:, 6 + u % 2, 0:nk]).then_inc(pT_rdy, 1)

                exp(0)
                for u in range(len(us)):
                    if u + 1 < len(us):
                        exp(u + 1)
                    pT_out(u)
                if n == 0:
                    root(oss[:])
                rows_out(co, oT_rdy)
                take(act, x_rdy, co)
                sumsq(co)
                root(ss[:, 0:co])
                for t in range(4):
                    tr_out(keysT[:, 4 * t:4 * t + 4, :].rearrange("p t n -> p (t n)"))
                act.drain().then_inc(keysT_rdy, 1)
                rows_out(co, hT_rdy)
                with act.Fori(0, 2) as i:
                    for t in range(8):
                        take(act, proj_rdy)
                        dst = big[:, bass.ds(i * 4096 + 9216 + t * 512, co * P)]
                        copy(dst, ps[:, t % 4, 0:co * P]).then_inc(bank_free[t % 4], 1)
                act.drain().then_inc(qry_rdy, 1)
                for t in range(4 * co):
                    take(act, sc_rdy)
                    copy(scores[:, t * 512:(t + 1) * 512], ps[:, 4 + t % 2, :]).then_inc(bank_free[4 + t % 2], 1)
                    if t == 3:
                        act.drain().then_inc(score_rdy, 1)
                act.drain().then_inc(score_rdy, 1)

                def weights_exp(par):
                    take(act, best_rdy)
                    nc.scalar.activation(gexp[:, par, :], best[:, par, :], ACT.Exp, bias=nbest[:, par:par + 1],
                                         accum_out=gsum[:, par:par + 1]).then_inc(gexp_rdy, 1)

                def gelu_tanh():
                    take(act, gz_rdy)
                    nc.scalar.activation(gth[:], gz[:], ACT.Tanh, scale=GELU_C).then_inc(gth_rdy, 1)

                def diagonals(par):
                    take(act, coef_rdy)
                    for k in range(TOPK):
                        take(act, diag_free)
                        nc.scalar.activation(diag[:, k % DIAGS, :], ident[:], ACT.Copy,
                                             scale=coef[:, par, k:k + 1]).then_inc(diag_rdy, 1)

                def step(par, topk, u, v):
                    if topk:
                        weights_exp(1 - par)
                    if v:
                        diagonals(1 - par)
                    if u:
                        gelu_tanh()

                if n == 0:
                    act.sem_inc(diag_free, DIAGS - 1)
                weights_exp(0)
                step(0, True, True, False)
                with act.Fori(0, (groups[n] - 2) // 2):
                    step(1, True, True, True)
                    step(0, True, True, True)
                step(1, False, True, True)
                step(0, False, False, True)

        @block.tensor
        def _(pe):
            bank = [0]
            for b in range(8):
                pe.sem_inc(bank_free[b], 1)
            for s in range(2):
                pe.sem_inc(w_free[s], 1)

            def transposes(srcs):
                b = 6 + bank[0] % 2
                bank[0] += 1
                take(pe, bank_free[b])
                for j, src in enumerate(srcs):
                    mm = nc.tensor.transpose(ps[:, b, j * P:(j + 1) * P], src, ident[:])
                mm.then_inc(tr_rdy, 1)

            def rows(src, chunks, rdy):
                for c in range(chunks):
                    take(pe, rdy)
                    for half in range(2):
                        transposes([src[:, c, (4 * half + j) * P:(4 * half + j + 1) * P] for j in range(4)])

            def project(slot, chunks, width, done):
                for c in chunks:
                    take(pe, bank_free[c])
                    for k in range(KD):
                        mm = nc.tensor.matmul(ps[:, c, 0:width], hT[:, k, c * P:(c + 1) * P],
                                              ring_w[:, slot, k, 0:width], start=(k == 0), stop=(k == KD - 1))
                    mm.then_inc(done, 1)
                pe.drain().then_inc(w_free[slot], 1)

            take(pe, cs_rdy)
            pe.wait_ge(const_in, 16 * 5)
            take(pe, bank_free[4])
            nc.tensor.transpose(ps[:, 4, 0:16], crow[:], ident[0:16, 0:16]).then_inc(ada_rdy, 1)
            take(pe, cT_rdy)
            for n in range(LAYERS):
                with pe.Fori(0, ADA_TILES // 2) as i:
                    for slot in range(2):
                        take(pe, bank_free[slot])
                        pe.wait_ge(w_in[slot], i * 16 + 16 * (n * ADA_W + 1))
                        for k in range(KD):
                            mm = nc.tensor.matmul(ps[0:2, slot, :], cT[:, k:16:8], ring_w[:, slot, k, :],
                                                  start=(k == 0), stop=(k == KD - 1))
                        mm.then_inc(ada_rdy, 1)
                        pe.drain().then_inc(w_free[slot], 1)

            for n in range(LAYERS):
                co = chunks_out[n]
                rows(h, NCH, h_rdy)
                take(pe, hT_rdy)
                width = in_width[n]
                for slot in range(2):
                    pe.wait_ge(w_in[slot], 16 * (wbase(n, 0) + 1))
                    project(slot, range(NCH if n == 0 else LAT), width, proj_rdy)
                with pe.Fori(0, 2) as i:
                    for slot in range(2):
                        pe.wait_ge(w_in[slot], i * 16 + 16 * (wbase(n, 0) + 2))
                        project(slot, range(NCH), width, proj_rdy)
                take(pe, qk_rdy)
                if n == 0:
                    for t in range(4):
                        transposes([big[:, qcol(0, c, t * P):qcol(0, c, t * P) + P] for c in range(NCH)])
                    take(pe, kdup_rdy)
                    for t in range(2):
                        transposes([kdup[:, c, t * P:(t + 1) * P] for c in range(NCH)])
                    take(pe, qk_rdy)
                    for t in range(8):
                        transposes([big[:, qcol(0, c, B_Q0 + t * P):qcol(0, c, B_Q0 + t * P) + P] for c in range(NCH)])
                else:
                    for t in range(8):
                        transposes([big[:, qcol(1, c, t * P):qcol(1, c, t * P) + P] for c in range(LAT)])
                    take(pe, qk_rdy)
                    for t in range(8):
                        transposes([big[:, qcol(1, c, D + t * P):qcol(1, c, D + t * P) + P] for c in range(NCH)])
                take(pe, qkT_rdy)
                us = units(n)
                for b in range(4, 8):
                    take(pe, bank_free[b])

                def score(u):
                    keyT, c0 = kT(n, us[u])
                    nc.tensor.matmul(ps[:, 4 + u % 2, 0:(NCH - c0) * P], qT(n, us[u]), keyT, start=True, stop=True)\
                        .then_inc(s_rdy, 1)

                def prob_T(u):
                    take(pe, p_rdy)
                    for j in range(NCH if us[u]["c"] < LAT else NCH - LAT):
                        mm = nc.tensor.transpose(ps[:, 6 + u % 2, j * P:(j + 1) * P],
                                                 prob[:, u % 2, j * P:(j + 1) * P], ident[:])
                    mm.then_inc(tr_rdy, 1)

                def values(u):
                    q = us[u]
                    b0 = 2 * (q["group"] % 2)
                    if q["first"]:
                        for b in (b0, b0 + 1):
                            take(pe, bank_free[b])
                    take(pe, pT_rdy)
                    c0 = 0 if q["c"] < LAT else LAT
                    for j in range(NCH - c0):
                        v0 = qcol(n, c0 + j, q["v"])
                        mm = nc.tensor.matmul(ps[:, b0 + q["bank"], q["col"]:q["col"] + q["w"]],
                                              probT[:, u % 2, j * P:(j + 1) * P], big[:, v0:v0 + q["w"]],
                                              start=(j == 0), stop=(c0 + j == NCH - 1))
                    if q["last"]:
                        mm.then_inc(o_rdy, 1)

                score(0)
                for u in range(len(us)):
                    if u + 1 < len(us):
                        score(u + 1)
                    prob_T(u)
                    if u:
                        values(u - 1)
                values(len(us) - 1)
                pe.drain().then_inc(own_t, 1)
                pe.wait_ge(own_t, n + 1)
                for b in range(4, 8):
                    pe.sem_inc(bank_free[b], 1)
                bank[0] = 0
                rows(o, co, on_rdy)
                take(pe, oT_rdy)
                for slot in range(2):
                    pe.wait_ge(w_in[slot], 16 * (wbase(n, 1) + 1))
                    project(slot, range(co), 512, op_rdy)
                pe.wait_ge(keys_in[n], 16)
                for t in range(4):
                    transposes([keys[:, 4 * t + j, :] for j in range(4)])
                rows(h, co, h_rdy)
                take(pe, hT_rdy)
                with pe.Fori(0, 2) as i:
                    for slot in range(2):
                        pe.wait_ge(w_in[slot], i * 16 + 16 * (wbase(n, 2) + 1))
                        for t in range(4):
                            take(pe, bank_free[t])
                            for k in range(KD):
                                mm = nc.tensor.matmul(ps[:, t, 0:co * P], ring_w[:, slot, k, t * P:(t + 1) * P],
                                                      hT[:, k, 0:co * P], start=(k == 0), stop=(k == KD - 1))
                            mm.then_inc(proj_rdy, 1)
                        pe.drain().then_inc(w_free[slot], 1)
                take(pe, qry_rdy)
                take(pe, keysT_rdy)
                for c in range(co):
                    for t in range(4):
                        take(pe, bank_free[4 + t % 2])
                        for j in range(4):
                            mm = nc.tensor.matmul(ps[:, 4 + t % 2, j * P:(j + 1) * P],
                                                  qryT[:, 4 * t + j, c * P:(c + 1) * P], keysT[:, 4 * t + j, :],
                                                  start=True, stop=True)
                        mm.then_inc(sc_rdy, 1)

                def expert_sum(base, i2):
                    for b in range(2):
                        take(pe, bank_free[b])
                    for k in range(TOPK):
                        take(pe, diag_rdy)
                        pe.wait_ge(v_in[k % RING], i2 + 16 * (base + k // RING + 1))
                        nc.tensor.matmul(ps[:, 0, :], diag[:, k % DIAGS, :], vring[k % RING][:, 0:512],
                                         start=(k == 0), stop=(k == TOPK - 1)).then_inc(diag_free, 1)
                        nc.tensor.matmul(ps[:, 1, :], diag[:, k % DIAGS, :], vring[k % RING][:, 512:1024],
                                         start=(k == 0), stop=(k == TOPK - 1)).then_inc(v_free, 1)
                    pe.drain().then_inc(y_rdy, 1)

                per = TOPK // RING
                base = per * sum(groups[:n])
                with pe.Fori(0, (groups[n] - 2) // 2) as i:
                    for j in range(2):
                        expert_sum(base + per * j, i * (16 * per * 2))
                for j in range(groups[n] - 2, groups[n]):
                    expert_sum(base + per * j, 0)

        @block.vector
        def _(dve):
            v = nc.vector
            own = Chain(dve, own_v)
            TT, STT, TS = v.tensor_tensor, v.scalar_tensor_tensor, v.tensor_scalar

            take(dve, silu_rdy)
            own.link(STT(crow[:], cth[:], 1.0, crow[:], ALU.add, ALU.mult))
            TS(crow[:], crow[:], 0.5, None, ALU.mult).then_inc(cs_rdy, 1)
            take(dve, ada_rdy)
            v.tensor_copy(cT[:], ps[:, 4, 0:16]).then_inc(cT_rdy, 1)
            for n in range(LAYERS):
                dve.wait_ge(adab_in[n], 16 * (3 if n == 0 else 2))
                tail = small[0:2, 0:2048] if n == 0 else small[0:2, 3072:5120]
                own.link(v.tensor_copy(modrow[n][:, 0:4096], adab[n][:, 0:4096]))
                own.link(v.tensor_copy(modrow[n][:, 4096:6144], tail))
                base = QKT0 if n == 0 else 0
                own.reset()
                with dve.Fori(0, ADA_TILES // 2) as i:
                    for slot in range(2):
                        take(dve, ada_rdy)
                        row = big[0:2, bass.ds(i * 1024 + base + slot * 512, 512)]
                        TT(row, ps[0:2, slot, :], row, ALU.add).then_inc(bank_free[slot], 1)
                dve.drain().then_inc(modrow_rdy, 1)
            dve.sem_inc(bank_free[4], 1)
            own.link(v.memset(pad, 0.0))
            dve.sem_inc(pad_rdy, 1)
            dve.wait_ge(const_in, 16 * 13)
            lv = lam_in[:].rearrange("p (a b n) -> p a b n", a=2, b=2)
            own.link(TT(lv[:, :, 0, :], lv[:, :, 0, :], lv[:, :, 1, :], ALU.mult))
            v.tensor_reduce(lam2[:], lv[:, :, 0, :], AX_X, ALU.add).then_inc(lam_rdy, 1)
            take(dve, lamx_rdy)
            own.link(TT(neg_lam[:], lam2[:, 1:2], lam2[:, 0:1], ALU.subtract))
            own.link(TS(neg_lam[:], neg_lam[:], -LAM_INIT, None, ALU.add))
            for g in (0, 2, 4):
                own.link(TS(gains[:, g, :], gains[:, g, :], HD ** -0.5, None, ALU.mult))
            own.link(TS(subln[:], subln[:], 1.0 - LAM_INIT, None, ALU.mult))

            def rms(sums, result, count, wait_ready=None):
                own.link(TS(sums, sums, 1.0 / count, EPS, ALU.mult, ALU.add))
                dve.sem_inc(sq_in, 1)
                take(dve, sq_rdy)
                own.link(v.reciprocal(result, sums))

            def row_norm(n, chunks, loaded, freed):
                dve.wait_ge(loaded, 16 * 3)
                for s in range(2):
                    own.link(STT(mb[:, s, 1, :], mb[:, s, 1, :], 1.0, grow[:], ALU.add, ALU.mult))
                take(dve, ss_rdy, chunks)
                rms(ss[:, 0:chunks], rstd[:, 0:chunks], D)
                for c in range(chunks):
                    s = 0 if c < LAT else 1
                    own.link(STT(h[:, c, :], xs[:, c, :], rstd[:, c:c + 1], mb[:, s, 1, :], ALU.mult, ALU.mult))
                    own.link(TT(h[:, c, :], h[:, c, :], mb[:, s, 0, :], ALU.add))
                    dve.sem_inc(h_rdy, 1)
                if freed is not None:
                    dve.sem_inc(freed, 1)

            def head_sums(n, chunks, col, heads):
                for c in range(chunks):
                    q0 = qcol(n, c, col)
                    x = big[:, q0:q0 + heads * HD]
                    own.link(TT(tmpA[:, 0:heads * HD], x, x, ALU.mult))
                    own.link(v.tensor_reduce(hss[:, c * heads:(c + 1) * heads],
                                             tmpA[:, 0:heads * HD].rearrange("p (h n) -> p h n", n=HD), AX_X, ALU.add))

            def head_scale(n, chunks, col, heads, gain_of):
                for c in range(chunks):
                    q0 = qcol(n, c, col)
                    x = big[:, q0:q0 + heads * HD].rearrange("p (h n) -> p h n", n=HD)
                    r = hrs[:, c * heads:(c + 1) * heads].unsqueeze(2).to_broadcast([P, heads, HD])
                    own.link(TT(x, x, r, ALU.mult))
                    for h0, h1, g in gain_of:
                        own.add(TT(x[:, h0:h1, :], x[:, h0:h1, :],
                                   gains[:, g, :].unsqueeze(1).to_broadcast([P, h1 - h0, HD]), ALU.mult))
                    own.wait()
                    if n == 0 and c < LAT:
                        t1 = tmpA[:, 0:heads * HD].rearrange("p (h n) -> p h n", n=HD)
                        own.add(TT(t1, x, rope_c[:, c, :].unsqueeze(1).to_broadcast([P, heads, HD]), ALU.mult))
                        xv = x.rearrange("p h (x f i) -> p h x f i", x=2, f=2)
                        tv = tmpB[:, 0:heads * HD].rearrange("p (h x f i) -> p h x f i", x=2, f=2, i=16)
                        sv = rope_s[:, c, :].rearrange("p (x f i) -> p x f i", x=2, f=2)
                        for f in range(2):
                            own.add(TT(tv[:, :, :, f, :], xv[:, :, :, 1 - f, :],
                                       sv[:, :, f, :].unsqueeze(1).to_broadcast([P, heads, 2, 16]), ALU.mult))
                        own.wait()
                        own.link(TT(x, t1, tmpB[:, 0:heads * HD].rearrange("p (h n) -> p h n", n=HD), ALU.add))

            dve.wait_ge(x_in, 32)
            dve.sem_inc(x_rdy, 1)
            for n in range(LAYERS):
                co = chunks_out[n]
                row_norm(n, NCH, mod01_in[n][0], mod01_free)
                take(dve, qkv_rdy)
                if n == 0:
                    head_sums(0, NCH, 0, 10)
                    rms(hss[:, 0:40], hrs[:, 0:40], HD)
                    head_scale(0, NCH, 0, 10, [(0, 8, 0), (8, 10, 1)])
                    dve.sem_inc(qk_rdy, 1)
                    dve.sem_inc(ka_rdy, 1)
                    take(dve, qkv_rdy)
                    head_sums(0, NCH, B_Q0, 16)
                    rms(hss[:], hrs[:], HD)
                    head_scale(0, NCH, B_Q0, 16, [(0, 8, 2), (8, 16, 3)])
                    dve.sem_inc(qk_rdy, 1)
                else:
                    head_sums(1, LAT, 0, 16)
                    rms(hss[:, 0:32], hrs[:, 0:32], HD)
                    head_scale(1, LAT, 0, 16, [(0, 16, 4)])
                    dve.sem_inc(qk_rdy, 1)
                    take(dve, qkv_rdy)
                    head_sums(1, NCH, D, 16)
                    rms(hss[:], hrs[:], HD)
                    head_scale(1, NCH, D, 16, [(0, 16, 5)])
                    dve.sem_inc(qk_rdy, 1)
                    dve.sem_inc(bias_free, BIAS_SLOTS)
                us = units(n)

                def row_max(u):
                    q = us[u]
                    nk = (NCH if q["c"] < LAT else NCH - LAT) * P
                    s = ps[:, 4 + u % 2, 0:nk]
                    if q["bias"] is not None:
                        b = bias[:, q["bias"] % BIAS_SLOTS, :]
                        if q["c"] == 0:
                            dve.wait_ge(bias_in[q["bias"] % BIAS_SLOTS], 32 * (q["bias"] // BIAS_SLOTS + 1))
                            b3 = b.rearrange("p (i c) -> p i c", i=6)
                            own.link(TT(b3, b3, win_mask[:].unsqueeze(1).to_broadcast([P, 6, GRID_W]), ALU.add))
                    take(dve, s_rdy)
                    if q["bias"] is not None:
                        first = (2 - 2 * q["c"]) * GRID_W
                        own.link(TT(s[:, 0:SEQ], s[:, 0:SEQ], b[:, first:first + SEQ], ALU.add))
                        if q["c"] == LAT - 1 and q["bias"] + BIAS_SLOTS < C_HEADS:
                            dve.sem_inc(bias_free, 1)
                    v.tensor_reduce(negmax[:, u:u + 1], s, AX_X, ALU.max, negate=True).then_inc(max_rdy, 1)

                def group_out(last):
                    q = us[last]
                    b0 = 2 * (q["group"] % 2)
                    take(dve, o_rdy)
                    if n == 0:
                        c = q["c"]
                        own.link(v.reciprocal(rinv[:, 0:8], rsum[:, last - 7:last + 1]))
                        if q["group"] < NCH:
                            own.link(TT(o[:, c, 0:512].rearrange("p (h n) -> p h n", n=HD),
                                        ps[:, b0, :].rearrange("p (h n) -> p h n", n=HD),
                                        rinv[:, 0:8].unsqueeze(2).to_broadcast([P, 8, HD]), ALU.mult))
                        else:
                            t = tmpA.rearrange("p (s n) -> p s n", n=2 * HD)
                            own.link(TT(t, ps[:, b0:b0 + 2, :].rearrange("p b (s n) -> p (b s) n", n=2 * HD),
                                        rinv[:, 0:8].unsqueeze(2).to_broadcast([P, 8, 2 * HD]), ALU.mult))
                            pair = tmpA.rearrange("p (s e n) -> p s e n", e=2, n=2 * HD)
                            d = o[:, c, 512:1024].rearrange("p (s n) -> p s n", n=2 * HD)
                            own.link(STT(d, pair[:, :, 1, :], neg_lam[:, 0:1], pair[:, :, 0, :], ALU.mult, ALU.add))
                            own.link(TT(tmpA[:, 0:512].rearrange("p (s n) -> p s n", n=2 * HD), d, d, ALU.mult))
                            own.link(v.tensor_reduce(oss[:, c * 4:c * 4 + 4],
                                                     tmpA[:, 0:512].rearrange("p (s n) -> p s n", n=2 * HD),
                                                     AX_X, ALU.add))
                    else:
                        own.link(v.reciprocal(rinv[:], rsum[:, last - 15:last + 1]))
                        r = rinv[:].rearrange("p (h c) -> p h c", c=2)
                        for c in range(LAT):
                            dst = o[:, c, q["group"] * 512:(q["group"] + 1) * 512].rearrange("p (h n) -> p h n", n=HD)
                            own.link(TT(dst, ps[:, b0 + c, :].rearrange("p (h n) -> p h n", n=HD),
                                        r[:, :, c].unsqueeze(2).to_broadcast([P, 8, HD]), ALU.mult))
                    for b in (b0, b0 + 1):
                        dve.sem_inc(bank_free[b], 1)

                due = []
                for u in range(len(us)):
                    row_max(u)
                    if due and u == due[0] + 3:
                        group_out(due.pop(0))
                    if us[u]["last"]:
                        due.append(u)
                group_out(due.pop(0))
                dve.sem_inc(keys_free, 1)
                if n == 0:
                    rms(oss[:], ors[:], 2 * HD)
                    for c in range(NCH):
                        d = o[:, c, 512:1024].rearrange("p (s n) -> p s n", n=2 * HD)
                        own.link(TT(d, d, ors[:, 4 * c:4 * c + 4].unsqueeze(2).to_broadcast([P, 4, 2 * HD]), ALU.mult))
                        own.link(TT(d, d, subln[:].unsqueeze(1).to_broadcast([P, 4, 2 * HD]), ALU.mult))
                        dve.sem_inc(on_rdy, 1)
                else:
                    dve.sem_inc(on_rdy, co)
                dve.wait_ge(mod2_in[n][0], 32)
                for t in range(2):
                    for c in range(co):
                        s = 0 if c < LAT else 1
                        cols = slice(t * 512, t * 512 + 512)
                        take(dve, op_rdy)
                        own.link(TT(ps[:, c, :], ps[:, c, :], mb[:, s, 2, cols], ALU.mult))
                        own.link(TT(xs[:, c, cols], xs[:, c, cols], ps[:, c, :], ALU.add))
                        dve.sem_inc(bank_free[c], 1)
                        if t == 1:
                            dve.sem_inc(x_rdy, 1)
                dve.sem_inc(mod2_free, 1)
                row_norm(n, co, mod01_in[n][1], None)

                def topk16(values, masked, vals, idx):
                    own.link(v.max(vals[:, 0:8], values))
                    own.add(v.max_index(idx[:, 0:8], vals[:, 0:8], values))
                    own.link(v.match_replace(masked, vals[:, 0:8], values, LOWEST))
                    own.link(v.max(vals[:, 8:16], masked))
                    own.link(v.max_index(idx[:, 8:16], vals[:, 8:16], masked))

                def select(i256, par):
                    own.link(v.tensor_copy(work.rearrange("p s n -> p (s n)"), scores[:, bass.ds(i256, 256)]))
                    for s in range(2):
                        topk16(work[:, s, :], work2[:, s, :], top[:, s, :], topi[:, s, :])
                    own.add(v.tensor_copy(topif[:], topi[:]))
                    c3 = cand.rearrange("p (i j) -> p i j", j=TOPK)
                    own.link(TT(c3, top[:, 0, :].unsqueeze(2).to_broadcast([P, TOPK, TOPK]),
                                top[:, 1, :].unsqueeze(1).to_broadcast([P, TOPK, TOPK]), ALU.add))
                    topk16(cand, cand2, best[:, par, :], bpos[:])
                    own.link(TS(nbest[:, par:par + 1], best[:, par, 0:1], -1.0, None, ALU.mult))
                    dve.sem_inc(best_rdy, 1)
                    own.add(TS(bij[:, 0, :], bpos[:], 4, None, ALU.logical_shift_right))
                    own.link(TS(bij[:, 1, :], bpos[:], TOPK - 1, None, ALU.bitwise_and))
                    own.link(v.tensor_copy(bijf[:], bij[:]))
                    hot = onehot.rearrange("p (s k j) -> p s k j", s=2, k=TOPK)
                    own.link(TT(hot, iota[:].unsqueeze(1).unsqueeze(1).to_broadcast([P, 2, TOPK, TOPK]),
                                bijf[:].unsqueeze(3).to_broadcast([P, 2, TOPK, TOPK]), ALU.is_equal))
                    own.link(TT(hot, hot, topif[:].unsqueeze(2).to_broadcast([P, 2, TOPK, TOPK]), ALU.mult))
                    own.link(v.tensor_reduce(seli[:].rearrange("p s k -> p (s k)"),
                                             onehot.rearrange("p (r j) -> p r j", j=TOPK), AX_X, ALU.add))
                    own.link(STT(expf[:, par, :], seli[:, 0, :], float(NKEYS), seli[:, 1, :], ALU.mult, ALU.add))
                    own.link(v.tensor_copy(idxu[:, par, :], expf[:, par, :]))
                    dve.sem_inc(idxu_rdy, 1)

                def step(par, i256, c_u, base, i_u, c_v, topk, u, vv):
                    if u:
                        v.tensor_copy(idxv[:, par, :], expf[:, par, :]).then_inc(idxv_rdy, 1)
                    if topk:
                        select(i256, 1 - par)
                    if u:
                        hrow = h[:].rearrange("p c n -> p (c n)")[:, bass.ds(c_u * D, D)]
                        for k in range(TOPK):
                            dve.wait_ge(u_in[k % RING], i_u + 16 * (base + k // RING + 1))
                            own.add(STT(uring[k % RING], uring[k % RING], 1.0, hrow, ALU.mult, ALU.mult,
                                        accum_out=dots[:, par, k:k + 1]))
                            if k:
                                dve.wait_ge(own_v, own.n - 1)
                                dve.sem_inc(u_free, 1)
                        own.wait()
                        dve.sem_inc(u_free, 1)
                        x = dots[:, par, :]
                        own.link(TT(gz[:], x, x, ALU.mult))
                        own.link(TS(gz[:], gz[:], 0.044715, 1.0, ALU.mult, ALU.add))
                        own.link(TT(gz[:], gz[:], x, ALU.mult))
                        dve.sem_inc(gz_rdy, 1)
                        take(dve, gexp_rdy)
                        own.link(v.reciprocal(ginv[:], gsum[:, par:par + 1]))
                        own.link(TT(gz2[:], x, gexp[:, par, :], ALU.mult))
                        own.link(TS(gz2[:], gz2[:], ginv[:, 0:1], 0.5, ALU.mult, ALU.mult))
                        take(dve, gth_rdy)
                        own.link(STT(coef[:, par, :], gth[:], 1.0, gz2[:], ALU.add, ALU.mult))
                        dve.sem_inc(coef_rdy, 1)
                    if vv:
                        take(dve, y_rdy)
                        yrow = y.rearrange("p c n -> p (c n)")[:, bass.ds(c_v * D, D)]
                        own.link(TT(yrow, ps[:, 0:2, :].rearrange("p b n -> p (b n)"), yrow, ALU.add))
                        for b in range(2):
                            dve.sem_inc(bank_free[b], 1)
                    own.reset()

                G = groups[n]
                per = TOPK // RING
                base = per * sum(groups[:n])
                take(dve, score_rdy)
                select(0, 0)
                take(dve, score_rdy)
                v.memset(y[:, 0:co, :], 0.0).then_inc(peer_go, 1)
                own.reset()
                step(0, 256, 0, base, 0, None, True, True, False)
                with dve.Fori(0, (G - 2) // 2) as i:
                    step(1, i * 512 + 512, i // 4, base + per, i * (32 * per), i // 4, True, True, True)
                    step(0, i * 512 + 768, (i + 1) // 4, base + 2 * per, i * (32 * per), i // 4, True, True, True)
                step(1, None, co - 1, base + per * (G - 1), 0, co - 1, False, True, True)
                step(0, None, None, base, 0, co - 1, False, False, True)
                dve.wait_ge(mod2_in[n][1], 32)
                for c in range(co):
                    s = 0 if c < LAT else 1
                    own.link(TT(y[:, c, :], y[:, c, :], mb[:, s, 2, :], ALU.mult))
                    own.link(TT(xs[:, c, :], xs[:, c, :], y[:, c, :], ALU.add))
                if n == 0:
                    dve.sem_inc(layer_done, 1)
                    dve.sem_inc(x_rdy, 1)
                else:
                    dve.sem_inc(x_out_rdy, 1)


def kernel(**inputs):
    import numpy as _np
    import concourse.bacc as _bacc
    from concourse import mybir as _mybir
    from concourse.bass_utils import run_bass_kernel_spmd as _run

    arrays = {k: _np.ascontiguousarray(v) for k, v in inputs.items()}
    for name in ("peer_u", "peer_v"):
        both = arrays.pop(name)
        for n in range(LAYERS):
            arrays[f"{name}{n}"] = _np.ascontiguousarray(both[n])
    rpb = arrays.pop("c_rpb")
    arrays["rpb_near"] = _np.ascontiguousarray(rpb[0][:, 4:4 + NEAR, :]).reshape(C_HEADS * NEAR, 31)
    arrays.update(constants())
    nc = _bacc.Bacc("TRN2", target_bir_lowering=False, num_devices=1)
    aps = {k: nc.dram_tensor(f"in_{k}", v.shape, _mybir.dt.from_np(v.dtype), kind="ExternalInput").ap()
           for k, v in arrays.items()}
    out = nc.dram_tensor("out_0", (1, SEQ, D), _mybir.dt.float32, kind="ExternalOutput").ap()
    build(nc, aps, out)
    r = _run(nc, [{f"in_{k}": v for k, v in arrays.items()}], core_ids=[0])
    return r.results[0]["out_0"]
```

```python
import math
from contextlib import ExitStack

import numpy as np

import concourse.bass as bass
from concourse import mybir

F32 = mybir.dt.float32
U32 = mybir.dt.uint32
ALU = mybir.AluOpType
ACT = mybir.ActivationFunctionType
AX_X = mybir.AxisListType.X

P = 128
D = 1024
KD = D // P
SEQ = 256
CTX_LEN = 256
LAT = SEQ // P
NCH = (SEQ + CTX_LEN) // P
LAYERS = 2
HD = 64
GRID_W = 64
EPS = 1e-6
A_HEADS, A_KV, B_HEADS = 8, 2, 4
AB_IN = 2304
A_K0, A_V0, B_Q0, B_K0, B_V0 = 512, 640, 768, 1280, 1792
C_HEADS = 16
NA_COLS = 16
HEADS, NKEYS, TOPK = 8, 128, 16
NEXP = NKEYS * NKEYS
LAM_INIT = 0.8 - 0.6 * math.exp(-0.3 * 0)
MASKED = -1.0e30
LOWEST = -3.0e38
GELU_C = math.sqrt(2.0 / math.pi)
LAG = 3
TURN = 4
RING = 8
RING0 = 4
DIAGS = 8
PARTS = 3
BIAS_SLOTS = 4
NEAR = 7
SKEW = 128


def constants():
    t = np.arange(SEQ)
    axis = HD // 2
    freqs = (1.0 / (10000.0 ** (np.arange(0, axis, 2, dtype=np.float32) / np.float32(axis)))).astype(np.float32)
    ang = np.stack([(t // GRID_W).astype(np.float32)[:, None] * freqs,
                    (t % GRID_W).astype(np.float32)[:, None] * freqs], 1)
    cos, sin = np.cos(ang).astype(np.float32), np.sin(ang).astype(np.float32)
    j = np.arange(GRID_W)
    start = np.clip(j - NA_COLS // 2, 0, GRID_W - NA_COLS)
    inside = (j[None] >= start[:, None]) & (j[None] < start[:, None] + NA_COLS)
    mask = np.where(inside, 0.0, MASKED).astype(np.float32)
    return {
        "ident": np.eye(P, dtype=np.float32),
        "iota": np.tile(np.arange(TOPK, dtype=np.float32), (P, 1)),
        "rope_c": np.stack([cos, cos], 2).reshape(SEQ, HD),
        "rope_s": np.stack([-sin, sin], 2).reshape(SEQ, HD),
        "win_mask": np.concatenate([mask, mask], 0),
    }


def take(eng, sem, n=1):
    eng.wait_ge(sem, n)
    eng.sem_inc(sem, -n)


class Chain:

    def __init__(self, eng, sem):
        self.eng, self.sem, self.n = eng, sem, 0

    def add(self, ins):
        ins.then_inc(self.sem, 1)
        self.n += 1

    def wait(self):
        self.eng.wait_ge(self.sem, self.n)

    def link(self, ins):
        self.add(ins)
        self.wait()

    def reset(self):
        self.wait()
        self.eng.sem_clear(self.sem)
        self.n = 0


def build(nc, a, out):
    ctx = ExitStack()
    with ctx:
        def sb(name, shape, dt=F32):
            return ctx.enter_context(nc.sbuf_tensor(name, shape, dt))

        def sem(name):
            return ctx.enter_context(nc.semaphore(name))

        xs = sb("xs", [P, NCH, D])
        mb = sb("mb", [P, 2, 3, D])
        grow = sb("grow", [P, D])
        h = sb("h", [P, NCH, D])
        o = h
        ring_w = sb("ring_w", [P, 2, KD, 512])
        hT = sb("hT", [P, KD, NCH * P])
        big = sb("big", [P, 17408])
        small = sb("small", [P, 5632])
        QKT0, QRY0 = 10240, 13312
        qkT = big[:, QKT0:QKT0 + 14 * 512].rearrange("p (t n) -> p t n", t=14)
        scores = big[:, 0:NCH * 2048]
        diag = big[:, 8192:8192 + DIAGS * P].rearrange("p (s n) -> p s n", s=DIAGS)
        qryT = big[:, QRY0:QRY0 + 2048].rearrange("p (t n) -> p t n", t=4)
        y = big[:, 9216:13312].rearrange("p (c n) -> p c n", c=NCH)
        tmpA = small[:, 0:1024]
        kdup = small[:, 1024:2048].rearrange("p (c n) -> p c n", c=NCH)
        prob = small[:, 2048:3072].rearrange("p (s n) -> p s n", s=2)
        tmpB = small[:, 2048:3072]
        probT = small[:, 3072:4096].rearrange("p (s n) -> p s n", s=2)
        bias = small[:, 4096:5632].rearrange("p (s n) -> p s n", s=BIAS_SLOTS)
        pad = small[0:C_HEADS * NEAR, 4352:4352 + SKEW]
        stage = small[0:2, 4608:5632].rearrange("p (s n) -> p s n", s=2)
        modrow = big[0:32, 9216:9216 + PARTS * P].rearrange("p (t n) -> p t n", t=PARTS)
        adab = big[0:32, 9216 + PARTS * P:9216 + 2 * PARTS * P].rearrange("p (t n) -> p t n", t=PARTS)
        lam_in = small[:, 4096:4096 + 4 * HD]
        keys = small[:, 0:2048].rearrange("p (t n) -> p t n", t=16)
        keysT = small[:, 2048:4096].rearrange("p (t n) -> p t n", t=16)
        work = small[:, 4096:4352].rearrange("p (s n) -> p s n", s=2)
        work2 = small[:, 4352:4608].rearrange("p (s n) -> p s n", s=2)
        cand = small[:, 4608:4864]
        cand2 = small[:, 4864:5120]
        onehot = small[:, 5120:5632]
        w_rows = [[ring_w[:, s, 2 * i:2 * i + 2, :].rearrange("p a b -> p (a b)") for i in range(4)]
                  for s in range(2)]
        uring = [mb[:, i // 2, i % 2, :] for i in range(RING0)] + w_rows[0]
        vring = [keys[:, 8 * i:8 * i + 8, :].rearrange("p t n -> p (t n)") for i in range(2)] + \
                [big[:, 15360 + 1024 * i:15360 + 1024 * (i + 1)] for i in range(2)] + w_rows[1]
        best, expf, gexp, dots, coef = [
            grow[:, k * TURN * TOPK:(k + 1) * TURN * TOPK].rearrange("p (b n) -> p b n", n=TOPK) for k in range(5)]
        crow = small[0:16, 0:P]
        cth = small[0:16, P:2 * P]

        ident = sb("ident", [P, P])
        iota = sb("iota", [P, TOPK])
        rope_c = sb("rope_c", [P, LAT, HD])
        rope_s = sb("rope_s", [P, LAT, HD])
        win_mask = sb("win_mask", [P, GRID_W])
        gains = sb("gains", [P, 6, HD])
        subln = sb("subln", [P, 2 * HD])
        lam2 = sb("lam2", [P, 2])
        neg_lam = sb("neg_lam", [P, 1])
        cT = sb("cT", [P, 16])
        ss = sb("ss", [P, NCH])
        rstd = sb("rstd", [P, NCH])
        hss = sb("hss", [P, NCH * 16])
        hrs = sb("hrs", [P, NCH * 16])
        negmax = sb("negmax", [P, 64])
        rsum = sb("rsum", [P, 64])
        rinv = sb("rinv", [P, 16])
        oss = sb("oss", [P, NCH * B_HEADS])
        ors = sb("ors", [P, NCH * B_HEADS])
        top = sb("top", [P, 2, TOPK])
        topi = sb("topi", [P, 2, TOPK], U32)
        topif = sb("topif", [P, 2, TOPK])
        bpos = sb("bpos", [P, TOPK], U32)
        bij = sb("bij", [P, 2, TOPK], U32)
        bijf = sb("bijf", [P, 2, TOPK])
        seli = sb("seli", [P, 2, TOPK])
        idxu = sb("idxu", [P, TURN, TOPK], U32)
        idxv = sb("idxv", [P, TURN, TOPK], U32)
        nbest = sb("nbest", [P, TURN])
        gsum = sb("gsum", [P, TURN])
        ginv = sb("ginv", [P, 1])
        gz = sb("gz", [P, TOPK])
        gz2 = sb("gz2", [P, TOPK])
        gth = sb("gth", [P, TOPK])
        ps = ctx.enter_context(nc.psum_tensor("ps", [P, 8, 512], F32))

        mod_dram = nc.dram_tensor("mod_scratch", [LAYERS, 2, 6 * D], F32, kind="Internal").ap()
        skew_dram = nc.dram_tensor("skew_scratch", [C_HEADS * NEAR, GRID_W, SKEW], F32, kind="Internal").ap()

        const_in = sem("const_in")
        c_in = sem("c_in")
        x_in = sem("x_in")
        adab_in = sem("adab_in")
        w_in = [sem(f"w_in{s}") for s in range(2)]
        mod_part = [sem(f"mod_part{s}") for s in range(2)]
        mod_out = [sem(f"mod_out{n}") for n in range(LAYERS)]
        mod01_in = [[sem(f"mod01_in{n}_{k}") for k in range(2)] for n in range(LAYERS)]
        mod2_in = [[sem(f"mod2_in{n}_{k}") for k in range(2)] for n in range(LAYERS)]
        pad_in = sem("pad_in")
        skew_out = sem("skew_out")
        bias_in = [sem(f"bias_in{s}") for s in range(BIAS_SLOTS)]
        keys_in = [sem(f"keys_in{n}") for n in range(LAYERS)]
        u_in = [sem(f"u_in{s}") for s in range(RING)]
        v_in = [sem(f"v_in{s}") for s in range(RING)]
        out_done = sem("out_done")
        w_free = [sem(f"w_free{s}") for s in range(2)]
        bank_free = [sem(f"bank_free{b}") for b in range(8)]
        mod01_free = sem("mod01_free")
        mod2_free = sem("mod2_free")
        bias_free = sem("bias_free")
        keys_free = sem("keys_free")
        w_rows_free = [sem(f"w_rows_free{s}") for s in range(2)]
        u_free = sem("u_free")
        v_free = sem("v_free")
        diag_free = sem("diag_free")
        modrow_rdy = sem("modrow_rdy")
        pad_rdy = sem("pad_rdy")
        silu_rdy = sem("silu_rdy")
        cs_rdy = sem("cs_rdy")
        cT_rdy = sem("cT_rdy")
        crT_rdy = sem("crT_rdy")
        ada_rdy = sem("ada_rdy")
        lam_rdy = sem("lam_rdy")
        lamx_rdy = sem("lamx_rdy")
        sq_in = sem("sq_in")
        sq_rdy = sem("sq_rdy")
        ss_rdy = sem("ss_rdy")
        x_rdy = sem("x_rdy")
        h_rdy = sem("h_rdy")
        tr_rdy = sem("tr_rdy")
        hT_rdy = sem("hT_rdy")
        proj_rdy = sem("proj_rdy")
        qkv_rdy = sem("qkv_rdy")
        qk_rdy = sem("qk_rdy")
        ka_rdy = sem("ka_rdy")
        kdup_rdy = sem("kdup_rdy")
        qkT_rdy = sem("qkT_rdy")
        s_rdy = sem("s_rdy")
        max_rdy = sem("max_rdy")
        p_rdy = sem("p_rdy")
        pT_rdy = sem("pT_rdy")
        o_rdy = sem("o_rdy")
        on_rdy = sem("on_rdy")
        oT_rdy = sem("oT_rdy")
        op_rdy = sem("op_rdy")
        keysT_rdy = sem("keysT_rdy")
        qry_rdy = sem("qry_rdy")
        sc_rdy = sem("sc_rdy")
        score_rdy = sem("score_rdy")
        peer_go = sem("peer_go")
        idxu_rdy = sem("idxu_rdy")
        idxv_rdy = sem("idxv_rdy")
        best_rdy = sem("best_rdy")
        gexp_rdy = sem("gexp_rdy")
        gz_rdy = sem("gz_rdy")
        gth_rdy = sem("gth_rdy")
        coef_rdy = sem("coef_rdy")
        diag_rdy = sem("diag_rdy")
        y_rdy = sem("y_rdy")
        layer_done = sem("layer_done")
        x_out_rdy = sem("x_out_rdy")
        own_v = sem("own_v")
        own_a = sem("own_a")
        own_t = sem("own_t")

        ADA_TILES = 6 * D // 512
        chunks_out = [NCH, LAT]
        groups = [n * HEADS for n in chunks_out]
        win = [a["ab_w_in"], a["c_w_in"]]
        wout = [a["ab_w_out"], a["c_w_out"]]
        in_width = [384, 512]
        ADA_BANK = (4, 5)
        ADA_GAPS = {"a": (0, 2), "b": (2, 8), "out": (8, 10), "norm2": (10, 12)}
        W_BEFORE = {(0, "ada"): 0, (0, "in"): 6, (1, "ada a"): 9, (1, "ada b"): 10, (1, "ada out"): 13,
                    (0, "out"): 14, (1, "ada norm2"): 15, (0, "query"): 16,
                    (1, "in"): 18, (1, "out"): 21, (1, "query"): 22}

        def tiles_before(n, stage):
            return W_BEFORE[n, stage]

        def qcol(n, c, col):
            if n == 0:
                return c * AB_IN + col
            return c * 3 * D + col if c < LAT else LAT * 3 * D + (c - LAT) * 2 * D + col - D

        def units(n):
            found = []
            if n == 0:
                for c in range(NCH):
                    for hh in range(A_HEADS):
                        found.append(dict(c=c, q=hh // 2, k=4 + hh // 4, half=hh % 2, v=A_V0 + HD * (hh // 4), w=HD,
                                          bank=0, col=hh * HD, bias=None, group=c, last=hh == A_HEADS - 1,
                                          first=hh == 0))
                for c in range(NCH):
                    for s in range(2 * B_HEADS):
                        found.append(dict(c=c, q=6 + s // 2, k=10 + s // 2, half=s % 2, v=B_V0 + 2 * HD * (s // 2),
                                          w=2 * HD, bank=s // 4, col=(s % 4) * 2 * HD, bias=None, group=NCH + c,
                                          last=s == 2 * B_HEADS - 1, first=s == 0))
            else:
                for hh in range(C_HEADS):
                    for c in range(LAT):
                        found.append(dict(c=c, q=hh // 2, k=8 + hh // 2, half=hh % 2, v=2 * D + HD * hh, w=HD,
                                          bank=c, col=(hh % 8) * HD, bias=hh, group=hh // 8,
                                          last=hh % 8 == 7 and c == 1, first=hh % 8 == 0 and c == 0))
            return found

        S_BANK = (4, 5, 7)
        PT_BANK = 6

        def u_landed(s, n, g, k):
            before = sum((LAG * TOPK // RING0 if s < RING0 else 0) + (G - LAG) * TOPK // RING for G in groups[:n])
            if g < LAG:
                return before + g * TOPK // RING0 + k // RING0 + 1
            return before + (LAG * TOPK // RING0 if s < RING0 else 0) + (g - LAG) * TOPK // RING + k // RING + 1

        def u_slot(g, k):
            return k % RING0 if g < LAG else (k + RING0) % RING

        def group_banks(n, u):
            b0 = 2 * (u["group"] % 2)
            return (b0,) if n == 0 and u["w"] == HD else (b0, b0 + 1)

        def kT(n, u):
            c0 = 0 if u["c"] < LAT else LAT
            rows = slice(HD * u["half"], HD * u["half"] + HD)
            if n == 0:
                return qkT[rows, u["k"], c0 * P:NCH * P], c0
            t = u["k"] - 8
            return cT_k[rows, t, :], 0

        cT_q = big[:, QKT0:QKT0 + 8 * 256].rearrange("p (t n) -> p t n", t=8)
        cT_k = big[:, QKT0 + 2048:QKT0 + 2048 + 8 * 512].rearrange("p (t n) -> p t n", t=8)

        def qT(n, u):
            rows = slice(HD * u["half"], HD * u["half"] + HD)
            cols = slice(u["c"] * P, u["c"] * P + P)
            return qkT[rows, u["q"], cols] if n == 0 else cT_q[rows, u["q"], cols]

        def spread(vec, n):
            return bass.AP(tensor=vec.tensor, offset=vec.offset, ap=[[0, P], [1, n]])

        block = ctx.enter_context(nc.Block())

        @block.sync
        def _(sp):
            sp.dma_start(crow[0:8, :], a["c"].rearrange("a (k p) -> (a k) p", p=P)).then_inc(c_in, 16)
            sp.dma_start(crow[8:16, :], a["c_ctx"].rearrange("(k p) -> k p", p=P)).then_inc(c_in, 16)
            consts = [(ident, a["ident"]), (iota, a["iota"]), (win_mask, a["win_mask"]),
                      (rope_c, a["rope_c"].rearrange("(c p) n -> p c n", p=P)),
                      (rope_s, a["rope_s"].rearrange("(c p) n -> p c n", p=P))]
            for dst, src in consts:
                sp.dma_start(dst[:], src).then_inc(const_in, 16)

            def load_adab(n):
                for s in range(2):
                    sp.dma_start(adab[16 * s:16 * s + 16, :, :], a["ada_b"][n].rearrange("(t j p) -> j t p", t=PARTS, p=P))\
                      .then_inc(adab_in, 16)

            load_adab(0)

            def load_tile(slot, src, width):
                take(sp, w_free[slot])
                sp.dma_start(ring_w[:, slot, :, 0:width], src).then_inc(w_in[slot], 16)

            def load_ada(n, first, last):
                src = a["ada_w"][n].rearrange("(k p) m -> p k m", p=P)
                with sp.Fori(first // 2, last // 2) as i:
                    for slot in range(2):
                        load_tile(slot, src[:, :, bass.ds(i * 1024 + slot * 512, 512)], 512)

            load_ada(0, 0, 2)
            sp.dma_start(xs[:, 0:LAT, :], a["x"][0].rearrange("(c p) n -> p c n", p=P)).then_inc(x_in, 16)
            sp.dma_start(xs[:, LAT:NCH, :], a["ctx"][0].rearrange("(c p) n -> p c n", p=P)).then_inc(x_in, 16)
            load_ada(0, 2, 6)
            small_in = [(gains[:, k, :], a[name][0]) for k, name in enumerate(
                ["a_q_norm", "a_k_norm", "b_q_norm", "b_k_norm", "c_q_norm", "c_k_norm"])]
            for dst, src in small_in:
                sp.dma_start(dst, spread(src, HD)).then_inc(const_in, 16)
            sp.dma_start(subln[:], spread(a["b_subln"], 2 * HD)).then_inc(const_in, 16)
            sp.dma_start(lam_in, spread(a["b_lambda"], 4 * HD)).then_inc(const_in, 16)

            def mod_to_dram(n, part):
                take(sp, modrow_rdy)
                for s in range(2):
                    sp.dma_start(mod_dram[n, s, part * 2 * D:(part + 1) * 2 * D].rearrange("(j p) -> j p", p=P),
                                 modrow[16 * s:16 * s + 16, part, :]).then_inc(mod_out[n], 16)
                sp.wait_ge(mod_out[n], 32 * (part + 1))

            def load_mod(n, first, rows, slot, done):
                for s in range(2):
                    src = mod_dram[n, s, first * D:(first + rows) * D]
                    sp.dma_start(mb[:, s, slot:slot + rows, :].rearrange("p r n -> p (r n)"),
                                 spread(src, rows * D)).then_inc(done, 16)

            for n in range(LAYERS):
                wi = win[n][0].rearrange("(k p) m -> p k m", p=P)
                width = in_width[n]
                if n == 1:
                    for slot in range(2):
                        load_tile(slot, wi[:, :, slot * width:(slot + 1) * width], width)
                    take(sp, layer_done)
                sp.dma_start(grow[:], spread(a["norm_g"][n, 0], D)).then_inc(mod01_in[n][0], 16)
                if n == 0:
                    mod_to_dram(0, 0)
                load_mod(n, 0, 2, 0, mod01_in[n][0])
                if n == 0:
                    load_ada(0, 6, ADA_TILES)
                    for slot in range(2):
                        load_tile(slot, wi[:, :, slot * width:(slot + 1) * width], width)
                    mod_to_dram(0, 1)
                load_mod(n, 2, 1, 2, mod2_in[n][0])
                if n == 0:
                    mod_to_dram(0, 2)
                    load_adab(1)
                take(sp, mod01_free)
                sp.dma_start(grow[:], spread(a["norm_g"][n, 1], D)).then_inc(mod01_in[n][1], 16)
                load_mod(n, 3, 2, 0, mod01_in[n][1])
                with sp.Fori(0, 2) as i:
                    for slot in range(2):
                        load_tile(slot, wi[:, :, bass.ds(i * (2 * width) + (2 + slot) * width, width)], width)
                if n == 0:
                    take(sp, pad_rdy)
                    sp.dma_start(pad[:, 48:48 + 31], a["rpb_near"]).then_inc(pad_in, 16)
                    sp.wait_ge(pad_in, 16)
                    sp.dma_start(skew_dram, bass.AP(tensor=pad.tensor, offset=pad.offset,
                                                    ap=[list(pad.ap[0]), [0, GRID_W], [1, SKEW]]))\
                      .then_inc(skew_out, 16)
                    load_ada(1, 0, ADA_GAPS["out"][1])
                    mod_to_dram(1, 0)
                    mod_to_dram(1, 1)
                wo = wout[n][0].rearrange("(k p) m -> p k m", p=P)
                for slot in range(2):
                    load_tile(slot, wo[:, :, slot * 512:(slot + 1) * 512], 512)
                if n == 0:
                    load_ada(1, *ADA_GAPS["norm2"])
                else:
                    for hh in range(C_HEADS):
                        take(sp, bias_free)
                        for odd in range(2):
                            src = bass.AP(tensor=skew_dram.tensor,
                                          offset=(hh * NEAR + 1 - odd) * GRID_W * SKEW + GRID_W - 1,
                                          ap=[[SKEW - 1, GRID_W], [GRID_W * SKEW, 6], [1, GRID_W]])
                            dst = bias[GRID_W * odd:GRID_W * odd + GRID_W, hh % BIAS_SLOTS, :]
                            sp.dma_start(dst.rearrange("p (i c) -> p i c", i=6), src)\
                              .then_inc(bias_in[hh % BIAS_SLOTS], 16)
                take(sp, keys_free)
                sp.dma_start(keys, a["peer_keys"][n].rearrange("h q n d -> n (h q) d")).then_inc(keys_in[n], 16)
                wq = a["peer_w_q"][n].rearrange("(k p) m -> p k m", p=P)
                with sp.Fori(0, 2) as i:
                    for slot in range(2):
                        load_tile(slot, wq[:, :, bass.ds(i * 1024 + slot * 512, 512)], 512)
                take(sp, mod2_free)
                load_mod(n, 5, 1, 2, mod2_in[n][1])
                if n == 0:
                    mod_to_dram(1, 2)
                    sp.wait_ge(skew_out, 16)
            take(sp, x_out_rdy)
            sp.dma_start(out[0].rearrange("(c p) n -> p c n", p=P), xs[:, 0:LAT, :]).then_inc(out_done, 16)
            sp.wait_ge(out_done, 16)

        @block.gpsimd
        def _(pool):
            def gather(table, idx, row, room, landed):
                take(pool, room)
                pool.indirect_dma_start(row, None, table, bass.IndirectOffsetOnAxis(idx, 0)).then_inc(landed, 16)

            def step(n, g, u=True, v=True):
                if u:
                    take(pool, idxu_rdy)
                if v:
                    take(pool, idxv_rdy)
                for k in range(TOPK):
                    if u:
                        s = u_slot(g, k)
                        gather(a[f"peer_u{n}"], idxu[:, g % TURN, k:k + 1], uring[s], u_free, u_in[s])
                    if v:
                        s = k % RING
                        gather(a[f"peer_v{n}"], idxv[:, (g - LAG) % TURN, k:k + 1], vring[s], v_free, v_in[s])

            for n in range(LAYERS):
                G = groups[n]
                take(pool, peer_go)
                pool.sem_inc(u_free, RING0)
                for g in range(LAG):
                    step(n, g, v=False)
                take(pool, w_rows_free[0])
                pool.sem_inc(u_free, RING - RING0)
                take(pool, w_rows_free[1])
                pool.sem_inc(v_free, RING)
                with pool.Fori(0, (G - 1 - LAG) // TURN):
                    for j in range(TURN):
                        step(n, LAG + j)
                step(n, G - 1)
                for g in range(G, G + LAG):
                    step(n, g, u=False)
                    if g == G:
                        take(pool, u_free, RING)
                        pool.sem_inc(w_free[0], 1)
                take(pool, v_free, RING)
                pool.sem_inc(w_free[1], 1)

        @block.scalar
        def _(act):
            bank = [0]
            own = Chain(act, own_a)

            def copy(dst, src):
                return nc.scalar.activation(dst, src, ACT.Copy)

            def tr_out(dst, width=512, shape=None):
                b = 6 + bank[0] % 2
                bank[0] += 1
                take(act, tr_rdy)
                src = ps[:, b, 0:width]
                if shape:
                    src = src.rearrange("p (t n) -> p t n", t=shape)
                copy(dst, src).then_inc(bank_free[b], 1)

            def rows_out(chunks, rdy):
                for c in range(chunks):
                    for half in range(2):
                        tr_out(hT[:, 4 * half:4 * half + 4, c * P:(c + 1) * P], shape=4)
                act.drain().then_inc(rdy, 1)

            def sumsq(chunks):
                for c in range(chunks):
                    nc.scalar.activation(h[:, c, :], xs[:, c, :], ACT.Square, accum_out=ss[:, c:c + 1])\
                      .then_inc(ss_rdy, 1)

            def root(t):
                take(act, sq_in)
                nc.scalar.activation(t, t, ACT.Sqrt).then_inc(sq_rdy, 1)

            def ada_out(n, t, part, turns=0):
                slot, T = t % 2, n * ADA_TILES + t
                if T >= 2:
                    act.wait_ge(mod_part[slot], turns + 32 * (T // 2))
                take(act, ada_rdy)
                own.add(copy(stage[:, slot, :], ps[0:2, ADA_BANK[slot], :]))
                own.wait()
                act.sem_inc(bank_free[ADA_BANK[slot]], 1)
                for s in range(2):
                    p0 = 16 * s + 4 * (t % 4)
                    act.dma_start(modrow[p0:p0 + 4, part, :], stage[s:s + 1, slot, :].rearrange("s (j p) -> s j p", p=P))\
                       .then_inc(mod_part[slot], 16)

            def ada_outs(gap):
                for t in range(*ADA_GAPS[gap]):
                    if t == 0:
                        act.wait_ge(mod_out[0], 32 * PARTS)
                    ada_out(1, t, t // 4)

            act.wait_ge(c_in, 32)
            nc.scalar.activation(cth[:], crow[:], ACT.Tanh, scale=0.5).then_inc(silu_rdy, 1)
            for t in range(4):
                ada_out(0, t, 0)
            for n in range(LAYERS):
                co = chunks_out[n]
                if n == 0:
                    act.wait_ge(x_in, 32)
                else:
                    take(act, x_rdy)
                sumsq(NCH)
                root(ss[:])
                if n == 0:
                    own.reset()
                    with act.Fori(0, PARTS - 1) as i:
                        for j in range(4):
                            ada_out(0, 4 + j, i + 1, i * 64)
                        own.reset()
                rows_out(NCH, hT_rdy)
                if n == 0:
                    take(act, lam_rdy)
                    nc.scalar.activation(lam2[:], lam2[:], ACT.Exp).then_inc(lamx_rdy, 1)
                width = in_width[n]
                first = NCH if n == 0 else LAT
                for t in range(2):
                    for c in range(first):
                        take(act, proj_rdy)
                        q0 = qcol(n, c, t * width)
                        copy(big[:, q0:q0 + width], ps[:, c, 0:width]).then_inc(bank_free[c], 1)
                act.drain().then_inc(qkv_rdy, 1)
                root(hss[:, 0:first * (10 if n == 0 else 16)])
                with act.Fori(0, 2) as i:
                    for t in range(2):
                        for c in range(NCH):
                            take(act, proj_rdy)
                            q0 = qcol(n, c, (2 + t) * width)
                            copy(big[:, bass.ds(i * (2 * width) + q0, width)], ps[:, c, 0:width])\
                                .then_inc(bank_free[c], 1)
                act.drain().then_inc(qkv_rdy, 1)
                if n == 0:
                    ada_outs("a")
                    take(act, ka_rdy)
                    for c in range(NCH):
                        q0 = qcol(0, c, A_K0)
                        src = big[:, q0:q0 + 2 * HD]
                        src = bass.AP(tensor=src.tensor, offset=src.offset,
                                      ap=[list(src.ap[0]), [HD, 2], [0, 2], [1, HD]])
                        copy(kdup[:, c, :].rearrange("p (a b n) -> p a b n", a=2, b=2), src)
                    act.drain().then_inc(kdup_rdy, 1)
                if n == 0:
                    for t in range(6):
                        tr_out(qkT[:, t, :])
                root(hss[:, 0:NCH * 16])
                if n == 0:
                    ada_outs("b")
                    for t in range(6, 14):
                        tr_out(qkT[:, t, :])
                else:
                    for t in range(8):
                        tr_out(cT_q[:, t, :], width=256)
                    for t in range(8):
                        tr_out(cT_k[:, t, :])
                act.drain().then_inc(qkT_rdy, 1)
                us = units(n)

                def exp(u):
                    nk = (NCH if us[u]["c"] < LAT else NCH - LAT) * P
                    take(act, max_rdy)
                    nc.scalar.activation(prob[:, u % 2, 0:nk], ps[:, S_BANK[u % 3], 0:nk], ACT.Exp,
                                         bias=negmax[:, u:u + 1], accum_out=rsum[:, u:u + 1]).then_inc(p_rdy, 1)

                def pT_out(u):
                    nk = (NCH if us[u]["c"] < LAT else NCH - LAT) * P
                    take(act, tr_rdy)
                    copy(probT[:, u % 2, 0:nk], ps[:, PT_BANK, 0:nk]).then_inc(pT_rdy, 1)

                exp(0)
                for u in range(len(us)):
                    if u + 1 < len(us):
                        exp(u + 1)
                    pT_out(u)
                if n == 0:
                    root(oss[:])
                    ada_outs("out")
                rows_out(co, oT_rdy)
                take(act, x_rdy, co)
                sumsq(co)
                root(ss[:, 0:co])
                for t in range(4):
                    tr_out(keysT[:, 4 * t:4 * t + 4, :].rearrange("p t n -> p (t n)"))
                act.drain().then_inc(keysT_rdy, 1)
                if n == 0:
                    ada_outs("norm2")
                rows_out(co, hT_rdy)
                def query_tile(t):
                    for j in range(4):
                        take(act, proj_rdy)
                        copy(qryT[:, j, 0:co * P], ps[:, 2 + j, 0:co * P]).then_inc(bank_free[2 + j], 1)
                    act.drain().then_inc(qry_rdy, 1)
                    for c in range(co):
                        take(act, sc_rdy)
                        s0 = (t * co + c) * 512
                        copy(scores[:, s0:s0 + 512], ps[:, 6 + c % 2, :]).then_inc(bank_free[6 + c % 2], 1)
                    act.drain().then_inc(score_rdy, 1)

                def weights_exp(g):
                    b = g % TURN
                    take(act, best_rdy)
                    nc.scalar.activation(gexp[:, b, :], best[:, b, :], ACT.Exp, bias=nbest[:, b:b + 1],
                                         accum_out=gsum[:, b:b + 1]).then_inc(gexp_rdy, 1)

                def diagonals(g):
                    take(act, coef_rdy)
                    for k in range(TOPK):
                        take(act, diag_free)
                        nc.scalar.activation(diag[:, k % DIAGS, :], ident[:], ACT.Copy,
                                             scale=coef[:, g % TURN, k:k + 1]).then_inc(diag_rdy, 1)

                def step(g, topk=True, u=True, v=True):
                    if topk:
                        weights_exp(g + 1)
                    if v:
                        diagonals(g - LAG)
                    if u:
                        take(act, gz_rdy)
                        nc.scalar.activation(gth[:], gz[:], ACT.Tanh, scale=GELU_C).then_inc(gth_rdy, 1)

                G = groups[n]
                if n == 0:
                    act.sem_inc(diag_free, DIAGS - 1)
                query_tile(0)
                weights_exp(0)
                for g in range(LAG):
                    query_tile(g + 1)
                    step(g, v=False)
                with act.Fori(0, (G - 1 - LAG) // TURN):
                    for j in range(TURN):
                        step(LAG + j)
                step(G - 1, topk=False)
                for g in range(G, G + LAG):
                    step(g, topk=False, u=False)

        @block.tensor
        def _(pe):
            bank = [0]
            for b in range(8):
                pe.sem_inc(bank_free[b], 1)
            for s in range(2):
                pe.sem_inc(w_free[s], 1)

            def transposes(srcs):
                b = 6 + bank[0] % 2
                bank[0] += 1
                take(pe, bank_free[b])
                for j, src in enumerate(srcs):
                    mm = nc.tensor.transpose(ps[:, b, j * P:(j + 1) * P], src, ident[:])
                mm.then_inc(tr_rdy, 1)

            def rows(src, chunks, rdy):
                for c in range(chunks):
                    take(pe, rdy)
                    for half in range(2):
                        transposes([src[:, c, (4 * half + j) * P:(4 * half + j + 1) * P] for j in range(4)])

            def project(slot, chunks, width, done):
                for c in chunks:
                    take(pe, bank_free[c])
                    for k in range(KD):
                        mm = nc.tensor.matmul(ps[:, c, 0:width], hT[:, k, c * P:(c + 1) * P],
                                              ring_w[:, slot, k, 0:width], start=(k == 0), stop=(k == KD - 1))
                    mm.then_inc(done, 1)
                pe.drain().then_inc(w_free[slot], 1)

            take(pe, cs_rdy)
            pe.wait_ge(const_in, 16 * 5)
            take(pe, bank_free[4])
            nc.tensor.transpose(ps[:, 4, 0:16], crow[:], ident[0:16, 0:16]).then_inc(crT_rdy, 1)
            take(pe, cT_rdy)

            def ada_tile(slot):
                take(pe, bank_free[ADA_BANK[slot]])
                for k in range(KD):
                    mm = nc.tensor.matmul(ps[0:2, ADA_BANK[slot], :], cT[:, k:16:8], ring_w[:, slot, k, :],
                                          start=(k == 0), stop=(k == KD - 1))
                mm.then_inc(ada_rdy, 1)
                pe.drain().then_inc(w_free[slot], 1)

            def ada_gap(gap):
                for t in range(*ADA_GAPS[gap]):
                    pe.wait_ge(w_in[t % 2], 16 * (tiles_before(1, "ada " + gap) + (t - ADA_GAPS[gap][0]) // 2 + 1))
                    ada_tile(t % 2)

            with pe.Fori(0, ADA_TILES // 2) as i:
                for slot in range(2):
                    pe.wait_ge(w_in[slot], i * 16 + 16)
                    ada_tile(slot)
            for n in range(LAYERS):
                co = chunks_out[n]
                rows(h, NCH, h_rdy)
                take(pe, hT_rdy)
                width = in_width[n]
                for slot in range(2):
                    pe.wait_ge(w_in[slot], 16 * (tiles_before(n, "in") + 1))
                    project(slot, range(NCH if n == 0 else LAT), width, proj_rdy)
                with pe.Fori(0, 2) as i:
                    for slot in range(2):
                        pe.wait_ge(w_in[slot], i * 16 + 16 * (tiles_before(n, "in") + 2))
                        project(slot, range(NCH), width, proj_rdy)
                if n == 0:
                    ada_gap("a")
                take(pe, qk_rdy)
                if n == 0:
                    for t in range(4):
                        transposes([big[:, qcol(0, c, t * P):qcol(0, c, t * P) + P] for c in range(NCH)])
                    take(pe, kdup_rdy)
                    for t in range(2):
                        transposes([kdup[:, c, t * P:(t + 1) * P] for c in range(NCH)])
                    ada_gap("b")
                    take(pe, qk_rdy)
                    for t in range(8):
                        transposes([big[:, qcol(0, c, B_Q0 + t * P):qcol(0, c, B_Q0 + t * P) + P] for c in range(NCH)])
                else:
                    for t in range(8):
                        transposes([big[:, qcol(1, c, t * P):qcol(1, c, t * P) + P] for c in range(LAT)])
                    take(pe, qk_rdy)
                    for t in range(8):
                        transposes([big[:, qcol(1, c, D + t * P):qcol(1, c, D + t * P) + P] for c in range(NCH)])
                take(pe, qkT_rdy)
                us = units(n)
                for b in range(4, 8):
                    take(pe, bank_free[b])

                def score(u):
                    keyT, c0 = kT(n, us[u])
                    nc.tensor.matmul(ps[:, S_BANK[u % 3], 0:(NCH - c0) * P], qT(n, us[u]), keyT, start=True, stop=True)\
                        .then_inc(s_rdy, 1)

                def prob_T(u):
                    take(pe, p_rdy)
                    if u:
                        take(pe, pT_rdy)
                    for j in range(NCH if us[u]["c"] < LAT else NCH - LAT):
                        mm = nc.tensor.transpose(ps[:, PT_BANK, j * P:(j + 1) * P],
                                                 prob[:, u % 2, j * P:(j + 1) * P], ident[:])
                    mm.then_inc(tr_rdy, 1)

                def values(u):
                    q = us[u]
                    b0 = 2 * (q["group"] % 2)
                    if q["first"]:
                        for b in group_banks(n, q):
                            take(pe, bank_free[b])
                    c0 = 0 if q["c"] < LAT else LAT
                    for j in range(NCH - c0):
                        v0 = qcol(n, c0 + j, q["v"])
                        mm = nc.tensor.matmul(ps[:, b0 + q["bank"], q["col"]:q["col"] + q["w"]],
                                              probT[:, u % 2, j * P:(j + 1) * P], big[:, v0:v0 + q["w"]],
                                              start=(j == 0), stop=(c0 + j == NCH - 1))
                    if q["last"]:
                        mm.then_inc(o_rdy, 1)

                for u in range(2):
                    score(u)
                for u in range(len(us)):
                    if u + 2 < len(us):
                        score(u + 2)
                    prob_T(u)
                    if u:
                        values(u - 1)
                take(pe, pT_rdy)
                values(len(us) - 1)
                pe.drain().then_inc(own_t, 1)
                pe.wait_ge(own_t, n + 1)
                for b in range(4, 8):
                    pe.sem_inc(bank_free[b], 1)
                bank[0] = 0
                if n == 0:
                    ada_gap("out")
                rows(o, co, on_rdy)
                take(pe, oT_rdy)
                for slot in range(2):
                    pe.wait_ge(w_in[slot], 16 * (tiles_before(n, "out") + 1))
                    project(slot, range(co), 512, op_rdy)
                pe.wait_ge(keys_in[n], 16)
                for t in range(4):
                    transposes([keys[:, 4 * t + j, :] for j in range(4)])
                if n == 0:
                    ada_gap("norm2")
                rows(h, co, h_rdy)
                take(pe, hT_rdy)
                take(pe, keysT_rdy)
                for t in range(4):
                    slot = t % 2
                    pe.wait_ge(w_in[slot], 16 * (tiles_before(n, "query") + t // 2 + 1))
                    for j in range(4):
                        take(pe, bank_free[2 + j])
                        for k in range(KD):
                            mm = nc.tensor.matmul(ps[:, 2 + j, 0:co * P], ring_w[:, slot, k, j * P:(j + 1) * P],
                                                  hT[:, k, 0:co * P], start=(k == 0), stop=(k == KD - 1))
                        mm.then_inc(proj_rdy, 1)
                    pe.drain().then_inc(w_free[slot] if t < 2 else w_rows_free[slot], 1)
                    take(pe, qry_rdy)
                    for c in range(co):
                        take(pe, bank_free[6 + c % 2])
                        for j in range(4):
                            mm = nc.tensor.matmul(ps[:, 6 + c % 2, j * P:(j + 1) * P],
                                                  qryT[:, j, c * P:(c + 1) * P], keysT[:, 4 * t + j, :],
                                                  start=True, stop=True)
                        mm.then_inc(sc_rdy, 1)

                def expert_sum(base, i2):
                    for b in range(2):
                        take(pe, bank_free[b])
                    for k in range(TOPK):
                        take(pe, diag_rdy)
                        pe.wait_ge(v_in[k % RING], i2 + 16 * (base + k // RING + 1))
                        nc.tensor.matmul(ps[:, 0, :], diag[:, k % DIAGS, :], vring[k % RING][:, 0:512],
                                         start=(k == 0), stop=(k == TOPK - 1)).then_inc(diag_free, 1)
                        nc.tensor.matmul(ps[:, 1, :], diag[:, k % DIAGS, :], vring[k % RING][:, 512:1024],
                                         start=(k == 0), stop=(k == TOPK - 1)).then_inc(v_free, 1)
                    pe.drain().then_inc(y_rdy, 1)

                per = TOPK // RING
                base = per * sum(groups[:n])
                turns = (groups[n] - 1 - LAG) // TURN
                with pe.Fori(0, turns) as i:
                    for j in range(TURN):
                        expert_sum(base + per * j, i * (16 * per * TURN))
                for j in range(turns * TURN, groups[n]):
                    expert_sum(base + per * j, 0)

        @block.vector
        def _(dve):
            v = nc.vector
            own = Chain(dve, own_v)
            TT, STT, TS = v.tensor_tensor, v.scalar_tensor_tensor, v.tensor_scalar

            take(dve, silu_rdy)
            own.link(STT(crow, cth, 1.0, crow, ALU.add, ALU.mult))
            TS(crow, crow, 0.5, None, ALU.mult).then_inc(cs_rdy, 1)
            take(dve, crT_rdy)
            own.link(v.tensor_copy(cT[:], ps[:, 4, 0:16]))
            dve.sem_inc(cT_rdy, 1)
            dve.sem_inc(bank_free[4], 1)

            def mod_rows_out(n, part):
                for slot in range(2):
                    dve.wait_ge(mod_part[slot], 32 * (n * ADA_TILES // 2 + 2 * (part + 1)))
                dve.wait_ge(adab_in, 32 * (n + 1))
                own.link(TT(modrow[:, part, :], modrow[:, part, :], adab[:, part, :], ALU.add))
                dve.sem_inc(modrow_rdy, 1)

            mod_rows_out(0, 0)

            def rms(sums, result, count, wait_ready=None):
                own.link(TS(sums, sums, 1.0 / count, EPS, ALU.mult, ALU.add))
                dve.sem_inc(sq_in, 1)
                take(dve, sq_rdy)
                own.link(v.reciprocal(result, sums))

            def row_norm(n, chunks, loaded, freed):
                take(dve, ss_rdy, chunks)
                rms(ss[:, 0:chunks], rstd[:, 0:chunks], D)
                dve.wait_ge(loaded, 16 * 3)
                for s in range(2):
                    own.link(STT(mb[:, s, 1, :], mb[:, s, 1, :], 1.0, grow[:], ALU.add, ALU.mult))
                for c in range(chunks):
                    s = 0 if c < LAT else 1
                    own.link(STT(h[:, c, :], xs[:, c, :], rstd[:, c:c + 1], mb[:, s, 1, :], ALU.mult, ALU.mult))
                    own.link(TT(h[:, c, :], h[:, c, :], mb[:, s, 0, :], ALU.add))
                    dve.sem_inc(h_rdy, 1)
                if freed is not None:
                    dve.sem_inc(freed, 1)

            def head_sums(n, chunks, col, heads):
                for c in range(chunks):
                    q0 = qcol(n, c, col)
                    x = big[:, q0:q0 + heads * HD]
                    own.link(TT(tmpA[:, 0:heads * HD], x, x, ALU.mult))
                    own.link(v.tensor_reduce(hss[:, c * heads:(c + 1) * heads],
                                             tmpA[:, 0:heads * HD].rearrange("p (h n) -> p h n", n=HD), AX_X, ALU.add))

            def head_scale(n, chunks, col, heads, gain_of):
                for c in range(chunks):
                    q0 = qcol(n, c, col)
                    x = big[:, q0:q0 + heads * HD].rearrange("p (h n) -> p h n", n=HD)
                    r = hrs[:, c * heads:(c + 1) * heads].unsqueeze(2).to_broadcast([P, heads, HD])
                    own.link(TT(x, x, r, ALU.mult))
                    for h0, h1, g in gain_of:
                        own.add(TT(x[:, h0:h1, :], x[:, h0:h1, :],
                                   gains[:, g, :].unsqueeze(1).to_broadcast([P, h1 - h0, HD]), ALU.mult))
                    own.wait()
                    if n == 0 and c < LAT:
                        t1 = tmpA[:, 0:heads * HD].rearrange("p (h n) -> p h n", n=HD)
                        own.add(TT(t1, x, rope_c[:, c, :].unsqueeze(1).to_broadcast([P, heads, HD]), ALU.mult))
                        xv = x.rearrange("p h (x f i) -> p h x f i", x=2, f=2)
                        tv = tmpB[:, 0:heads * HD].rearrange("p (h x f i) -> p h x f i", x=2, f=2, i=16)
                        sv = rope_s[:, c, :].rearrange("p (x f i) -> p x f i", x=2, f=2)
                        for f in range(2):
                            own.add(TT(tv[:, :, :, f, :], xv[:, :, :, 1 - f, :],
                                       sv[:, :, f, :].unsqueeze(1).to_broadcast([P, heads, 2, 16]), ALU.mult))
                        own.wait()
                        own.link(TT(x, t1, tmpB[:, 0:heads * HD].rearrange("p (h n) -> p h n", n=HD), ALU.add))

            dve.wait_ge(x_in, 32)
            for n in range(LAYERS):
                co = chunks_out[n]
                row_norm(n, NCH, mod01_in[n][0], mod01_free)
                if n == 0:
                    mod_rows_out(0, 1)
                    mod_rows_out(0, 2)
                    own.link(v.memset(pad, 0.0))
                    dve.sem_inc(pad_rdy, 1)
                    dve.wait_ge(const_in, 16 * 13)
                    lv = lam_in.rearrange("p (a b n) -> p a b n", a=2, b=2)
                    own.link(TT(lv[:, :, 0, :], lv[:, :, 0, :], lv[:, :, 1, :], ALU.mult))
                    v.tensor_reduce(lam2[:], lv[:, :, 0, :], AX_X, ALU.add).then_inc(lam_rdy, 1)
                    take(dve, lamx_rdy)
                    own.link(TT(neg_lam[:], lam2[:, 1:2], lam2[:, 0:1], ALU.subtract))
                    own.link(TS(neg_lam[:], neg_lam[:], -LAM_INIT, None, ALU.add))
                    for g in (0, 2, 4):
                        own.link(TS(gains[:, g, :], gains[:, g, :], HD ** -0.5, None, ALU.mult))
                    own.link(TS(subln[:], subln[:], 1.0 - LAM_INIT, None, ALU.mult))

                take(dve, qkv_rdy)
                if n == 0:
                    head_sums(0, NCH, 0, 10)
                    rms(hss[:, 0:40], hrs[:, 0:40], HD)
                    head_scale(0, NCH, 0, 10, [(0, 8, 0), (8, 10, 1)])
                    dve.sem_inc(qk_rdy, 1)
                    dve.sem_inc(ka_rdy, 1)
                    take(dve, qkv_rdy)
                    head_sums(0, NCH, B_Q0, 16)
                    rms(hss[:], hrs[:], HD)
                    head_scale(0, NCH, B_Q0, 16, [(0, 8, 2), (8, 16, 3)])
                    dve.sem_inc(qk_rdy, 1)
                else:
                    head_sums(1, LAT, 0, 16)
                    rms(hss[:, 0:32], hrs[:, 0:32], HD)
                    head_scale(1, LAT, 0, 16, [(0, 16, 4)])
                    dve.sem_inc(qk_rdy, 1)
                    take(dve, qkv_rdy)
                    head_sums(1, NCH, D, 16)
                    rms(hss[:], hrs[:], HD)
                    head_scale(1, NCH, D, 16, [(0, 16, 5)])
                    dve.sem_inc(qk_rdy, 1)
                    dve.sem_inc(bias_free, BIAS_SLOTS)
                us = units(n)

                def row_max(u):
                    q = us[u]
                    nk = (NCH if q["c"] < LAT else NCH - LAT) * P
                    s = ps[:, S_BANK[u % 3], 0:nk]
                    if q["bias"] is not None:
                        b = bias[:, q["bias"] % BIAS_SLOTS, :]
                        if q["c"] == 0:
                            dve.wait_ge(bias_in[q["bias"] % BIAS_SLOTS], 32 * (q["bias"] // BIAS_SLOTS + 1))
                            b3 = b.rearrange("p (i c) -> p i c", i=6)
                            own.link(TT(b3, b3, win_mask[:].unsqueeze(1).to_broadcast([P, 6, GRID_W]), ALU.add))
                    take(dve, s_rdy)
                    if q["bias"] is not None:
                        first = (2 - 2 * q["c"]) * GRID_W
                        own.link(TT(s[:, 0:SEQ], s[:, 0:SEQ], b[:, first:first + SEQ], ALU.add))
                        if q["c"] == LAT - 1 and q["bias"] + BIAS_SLOTS < C_HEADS:
                            dve.sem_inc(bias_free, 1)
                    v.tensor_reduce(negmax[:, u:u + 1], s, AX_X, ALU.max, negate=True).then_inc(max_rdy, 1)

                def group_out(last):
                    q = us[last]
                    b0 = 2 * (q["group"] % 2)
                    take(dve, o_rdy)
                    if n == 0:
                        c = q["c"]
                        own.link(v.reciprocal(rinv[:, 0:8], rsum[:, last - 7:last + 1]))
                        if q["group"] < NCH:
                            own.link(TT(o[:, c, 0:512].rearrange("p (h n) -> p h n", n=HD),
                                        ps[:, b0, :].rearrange("p (h n) -> p h n", n=HD),
                                        rinv[:, 0:8].unsqueeze(2).to_broadcast([P, 8, HD]), ALU.mult))
                        else:
                            t = tmpA.rearrange("p (s n) -> p s n", n=2 * HD)
                            own.link(TT(t, ps[:, b0:b0 + 2, :].rearrange("p b (s n) -> p (b s) n", n=2 * HD),
                                        rinv[:, 0:8].unsqueeze(2).to_broadcast([P, 8, 2 * HD]), ALU.mult))
                            pair = tmpA.rearrange("p (s e n) -> p s e n", e=2, n=2 * HD)
                            d = o[:, c, 512:1024].rearrange("p (s n) -> p s n", n=2 * HD)
                            own.link(STT(d, pair[:, :, 1, :], neg_lam[:, 0:1], pair[:, :, 0, :], ALU.mult, ALU.add))
                            own.link(TT(tmpA[:, 0:512].rearrange("p (s n) -> p s n", n=2 * HD), d, d, ALU.mult))
                            own.link(v.tensor_reduce(oss[:, c * 4:c * 4 + 4],
                                                     tmpA[:, 0:512].rearrange("p (s n) -> p s n", n=2 * HD),
                                                     AX_X, ALU.add))
                    else:
                        own.link(v.reciprocal(rinv[:], rsum[:, last - 15:last + 1]))
                        r = rinv[:].rearrange("p (h c) -> p h c", c=2)
                        for c in range(LAT):
                            dst = o[:, c, q["group"] * 512:(q["group"] + 1) * 512].rearrange("p (h n) -> p h n", n=HD)
                            own.link(TT(dst, ps[:, b0 + c, :].rearrange("p (h n) -> p h n", n=HD),
                                        r[:, :, c].unsqueeze(2).to_broadcast([P, 8, HD]), ALU.mult))
                    for b in group_banks(n, q):
                        dve.sem_inc(bank_free[b], 1)

                due = []
                for u in range(len(us)):
                    row_max(u)
                    if due and u == due[0] + 3:
                        group_out(due.pop(0))
                    if us[u]["last"]:
                        due.append(u)
                    if n == 0 and u == A_HEADS:
                        mod_rows_out(1, 0)
                        mod_rows_out(1, 1)
                group_out(due.pop(0))
                dve.sem_inc(keys_free, 1)
                if n == 0:
                    rms(oss[:], ors[:], 2 * HD)
                    for c in range(NCH):
                        d = o[:, c, 512:1024].rearrange("p (s n) -> p s n", n=2 * HD)
                        own.link(TT(d, d, ors[:, 4 * c:4 * c + 4].unsqueeze(2).to_broadcast([P, 4, 2 * HD]), ALU.mult))
                        own.link(TT(d, d, subln[:].unsqueeze(1).to_broadcast([P, 4, 2 * HD]), ALU.mult))
                        dve.sem_inc(on_rdy, 1)
                else:
                    dve.sem_inc(on_rdy, co)
                dve.wait_ge(mod2_in[n][0], 32)
                for t in range(2):
                    for c in range(co):
                        s = 0 if c < LAT else 1
                        cols = slice(t * 512, t * 512 + 512)
                        take(dve, op_rdy)
                        own.link(TT(ps[:, c, :], ps[:, c, :], mb[:, s, 2, cols], ALU.mult))
                        own.link(TT(xs[:, c, cols], xs[:, c, cols], ps[:, c, :], ALU.add))
                        dve.sem_inc(bank_free[c], 1)
                        if t == 1:
                            dve.sem_inc(x_rdy, 1)
                dve.sem_inc(mod2_free, 1)
                row_norm(n, co, mod01_in[n][1], None)

                def topk16(values, masked, vals, idx):
                    own.link(v.max(vals[:, 0:8], values))
                    own.add(v.max_index(idx[:, 0:8], vals[:, 0:8], values))
                    own.link(v.match_replace(masked, vals[:, 0:8], values, LOWEST))
                    own.link(v.max(vals[:, 8:16], masked))
                    own.link(v.max_index(idx[:, 8:16], vals[:, 8:16], masked))

                def select(col, b):
                    own.link(v.tensor_copy(work.rearrange("p s n -> p (s n)"), scores[:, bass.ds(col, 256)]))
                    for s in range(2):
                        topk16(work[:, s, :], work2[:, s, :], top[:, s, :], topi[:, s, :])
                    own.add(v.tensor_copy(topif[:], topi[:]))
                    c3 = cand.rearrange("p (i j) -> p i j", j=TOPK)
                    own.link(TT(c3, top[:, 0, :].unsqueeze(2).to_broadcast([P, TOPK, TOPK]),
                                top[:, 1, :].unsqueeze(1).to_broadcast([P, TOPK, TOPK]), ALU.add))
                    topk16(cand, cand2, best[:, b, :], bpos[:])
                    own.link(TS(nbest[:, b:b + 1], best[:, b, 0:1], -1.0, None, ALU.mult))
                    dve.sem_inc(best_rdy, 1)
                    own.add(TS(bij[:, 0, :], bpos[:], 4, None, ALU.logical_shift_right))
                    own.link(TS(bij[:, 1, :], bpos[:], TOPK - 1, None, ALU.bitwise_and))
                    own.link(v.tensor_copy(bijf[:], bij[:]))
                    hot = onehot.rearrange("p (s k j) -> p s k j", s=2, k=TOPK)
                    own.link(TT(hot, iota[:].unsqueeze(1).unsqueeze(1).to_broadcast([P, 2, TOPK, TOPK]),
                                bijf[:].unsqueeze(3).to_broadcast([P, 2, TOPK, TOPK]), ALU.is_equal))
                    own.link(TT(hot, hot, topif[:].unsqueeze(2).to_broadcast([P, 2, TOPK, TOPK]), ALU.mult))
                    own.link(v.tensor_reduce(seli[:].rearrange("p s k -> p (s k)"),
                                             onehot.rearrange("p (r j) -> p r j", j=TOPK), AX_X, ALU.add))
                    own.link(STT(expf[:, b, :], seli[:, 0, :], float(NKEYS), seli[:, 1, :], ALU.mult, ALU.add))
                    own.link(v.tensor_copy(idxu[:, b, :], expf[:, b, :]))
                    dve.sem_inc(idxu_rdy, 1)

                def step(g, u_from=0, select_col=None, c_u=None, c_v=None):
                    if g >= LAG - 1:
                        b = (g + 1 - LAG) % TURN
                        v.tensor_copy(idxv[:, b, :], expf[:, b, :]).then_inc(idxv_rdy, 1)
                    if select_col is not None:
                        select(select_col, (g + 1) % TURN)
                    if c_u is not None:
                        b = g % TURN
                        hrow = h[:].rearrange("p c n -> p (c n)")[:, bass.ds(c_u * D, D)]
                        for k in range(TOPK):
                            s = u_slot(g, k)
                            dve.wait_ge(u_in[s], u_from + 16 * u_landed(s, n, g, k))
                            own.add(STT(uring[s], uring[s], 1.0, hrow, ALU.mult, ALU.mult,
                                        accum_out=dots[:, b, k:k + 1]))
                            if k:
                                dve.wait_ge(own_v, own.n - 1)
                                dve.sem_inc(u_free, 1)
                        own.wait()
                        dve.sem_inc(u_free, 1)
                        x = dots[:, b, :]
                        own.link(TT(gz[:], x, x, ALU.mult))
                        own.link(TS(gz[:], gz[:], 0.044715, 1.0, ALU.mult, ALU.add))
                        own.link(TT(gz[:], gz[:], x, ALU.mult))
                        dve.sem_inc(gz_rdy, 1)
                        take(dve, gexp_rdy)
                        own.link(v.reciprocal(ginv[:], gsum[:, b:b + 1]))
                        own.link(TT(gz2[:], x, gexp[:, b, :], ALU.mult))
                        own.link(TS(gz2[:], gz2[:], ginv[:, 0:1], 0.5, ALU.mult, ALU.mult))
                        take(dve, gth_rdy)
                        own.link(STT(coef[:, b, :], gth[:], 1.0, gz2[:], ALU.add, ALU.mult))
                        dve.sem_inc(coef_rdy, 1)
                    if c_v is not None:
                        take(dve, y_rdy)
                        yrow = y.rearrange("p c n -> p (c n)")[:, bass.ds(c_v * D, D)]
                        own.link(TT(yrow, ps[:, 0:2, :].rearrange("p b n -> p (b n)"), yrow, ALU.add))
                        for b in range(2):
                            dve.sem_inc(bank_free[b], 1)
                    own.reset()

                if n == 0:
                    mod_rows_out(1, 2)
                    dve.wait_ge(mod_out[1], 32 * PARTS)
                    dve.wait_ge(skew_out, 16)
                G = groups[n]
                own.link(v.memset(y[:, 0:co, :], 0.0))
                take(dve, score_rdy)
                dve.sem_inc(peer_go, 1)
                select(0, 0)
                own.reset()
                for g in range(LAG):
                    step(g, 0, (g + 1) * 256, g // 2 % co)
                take(dve, score_rdy, 3)
                with dve.Fori(0, (G - 1 - LAG) // TURN) as i:
                    for j in range(TURN):
                        g = LAG + j
                        step(g, i * (16 * TOPK // RING * TURN), i * (256 * TURN) + (g + 1) * 256,
                             (i * 2 + g // 2) % co, (i * 2 + j // 2) % co)
                step(G - 1, 0, None, (G - 1) // 2 % co, (G - 1 - LAG) // 2 % co)
                for g in range(G, G + LAG):
                    if g < G + LAG - 1:
                        step(g, c_v=(g - LAG) // 2 % co)
                    else:
                        step(-1, c_v=(g - LAG) // 2 % co)
                dve.wait_ge(mod2_in[n][1], 32)
                for c in range(co):
                    s = 0 if c < LAT else 1
                    own.link(TT(y[:, c, :], y[:, c, :], mb[:, s, 2, :], ALU.mult))
                    own.link(TT(xs[:, c, :], xs[:, c, :], y[:, c, :], ALU.add))
                if n == 0:
                    dve.sem_inc(layer_done, 1)
                    dve.sem_inc(x_rdy, 1)
                else:
                    dve.sem_inc(x_out_rdy, 1)


def kernel(**inputs):
    import numpy as _np
    import concourse.bacc as _bacc
    from concourse import mybir as _mybir
    from concourse.bass_utils import run_bass_kernel_spmd as _run

    arrays = {k: _np.ascontiguousarray(v) for k, v in inputs.items()}
    for name in ("peer_u", "peer_v"):
        both = arrays.pop(name)
        for n in range(LAYERS):
            arrays[f"{name}{n}"] = _np.ascontiguousarray(both[n])
    rpb = arrays.pop("c_rpb")
    arrays["rpb_near"] = _np.ascontiguousarray(rpb[0][:, 4:4 + NEAR, :]).reshape(C_HEADS * NEAR, 31)
    arrays.update(constants())
    nc = _bacc.Bacc("TRN2", target_bir_lowering=False, num_devices=1)
    aps = {k: nc.dram_tensor(f"in_{k}", v.shape, _mybir.dt.from_np(v.dtype), kind="ExternalInput").ap()
           for k, v in arrays.items()}
    out = nc.dram_tensor("out_0", (1, SEQ, D), _mybir.dt.float32, kind="ExternalOutput").ap()
    build(nc, aps, out)
    r = _run(nc, [{f"in_{k}": v for k, v in arrays.items()}], core_ids=[0])
    return r.results[0]["out_0"]
```

```python
import math
from contextlib import ExitStack

import numpy as np

import concourse.bass as bass
from concourse import mybir

F32 = mybir.dt.float32
U32 = mybir.dt.uint32
ALU = mybir.AluOpType
ACT = mybir.ActivationFunctionType
AX_X = mybir.AxisListType.X

P = 128
D = 1024
KD = D // P
SEQ = 256
CTX_LEN = 256
LAT = SEQ // P
NCH = (SEQ + CTX_LEN) // P
LAYERS = 2
HD = 64
GRID_W = 64
EPS = 1e-6
A_HEADS, A_KV, B_HEADS = 8, 2, 4
AB_IN = 2304
A_K0, A_V0, B_Q0, B_K0, B_V0 = 512, 640, 768, 1280, 1792
C_HEADS = 16
NA_COLS = 16
HEADS, NKEYS, TOPK = 8, 128, 16
LAM_INIT = 0.8 - 0.6 * math.exp(-0.3 * 0)
MASKED = -1.0e30
LOWEST = -3.0e38
GELU_C = math.sqrt(2.0 / math.pi)
LAG = 2
TURN = 4
RING = 8
RING0 = 4
SMALL = 2
DIAGS = 8
PARTS = 3
BIAS_SLOTS = 4
NEAR = 7
SKEW = 128


def constants():
    t = np.arange(SEQ)
    axis = HD // 2
    freqs = (1.0 / (10000.0 ** (np.arange(0, axis, 2, dtype=np.float32) / np.float32(axis)))).astype(np.float32)
    ang = np.stack([(t // GRID_W).astype(np.float32)[:, None] * freqs,
                    (t % GRID_W).astype(np.float32)[:, None] * freqs], 1)
    cos, sin = np.cos(ang).astype(np.float32), np.sin(ang).astype(np.float32)
    j = np.arange(GRID_W)
    start = np.clip(j - NA_COLS // 2, 0, GRID_W - NA_COLS)
    inside = (j[None] >= start[:, None]) & (j[None] < start[:, None] + NA_COLS)
    mask = np.where(inside, 0.0, MASKED).astype(np.float32)
    return {
        "ident": np.eye(P, dtype=np.float32),
        "iota": np.tile(np.arange(TOPK, dtype=np.float32), (P, 1)),
        "rope_c": np.stack([cos, cos], 2).reshape(SEQ, HD),
        "rope_s": np.stack([-sin, sin], 2).reshape(SEQ, HD),
        "win_mask": np.concatenate([mask, mask], 0),
    }


def take(eng, sem, n=1):
    eng.wait_ge(sem, n)
    eng.sem_inc(sem, -n)


class Chain:

    def __init__(self, eng, sem):
        self.eng, self.sem, self.n = eng, sem, 0

    def add(self, ins):
        ins.then_inc(self.sem, 1)
        self.n += 1

    def wait(self):
        self.eng.wait_ge(self.sem, self.n)

    def link(self, ins):
        self.add(ins)
        self.wait()

    def reset(self):
        self.wait()
        self.eng.sem_clear(self.sem)
        self.n = 0


def build(nc, a, out):
    ctx = ExitStack()
    with ctx:
        def sb(name, shape, dt=F32):
            return ctx.enter_context(nc.sbuf_tensor(name, shape, dt))

        def sem(name):
            return ctx.enter_context(nc.semaphore(name))

        xs = sb("xs", [P, NCH, D])
        mb = sb("mb", [P, 2, 3, D])
        grow = sb("grow", [P, D])
        h = sb("h", [P, NCH, D])
        o = h
        ring_w = sb("ring_w", [P, 2, KD, 512])
        hT = sb("hT", [P, KD, NCH * P])
        big = sb("big", [P, 17408])
        small = sb("small", [P, 5632])
        QKT0, QRY0 = 10240, 13312
        qkT = big[:, QKT0:QKT0 + 14 * 512].rearrange("p (t n) -> p t n", t=14)
        scores = big[:, 0:NCH * 2048]
        diag = big[:, 8192:8192 + DIAGS * P].rearrange("p (s n) -> p s n", s=DIAGS)
        qryT = big[:, QRY0:QRY0 + 2048].rearrange("p (t n) -> p t n", t=4)
        y = big[:, 9216:13312].rearrange("p (c n) -> p c n", c=NCH)
        tmpA = small[:, 0:1024]
        kdup = small[:, 1024:2048].rearrange("p (c n) -> p c n", c=NCH)
        prob = small[:, 2048:3072].rearrange("p (s n) -> p s n", s=2)
        tmpB = small[:, 2048:3072]
        probT = small[:, 3072:4096].rearrange("p (s n) -> p s n", s=2)
        bias = small[:, 4096:5632].rearrange("p (s n) -> p s n", s=BIAS_SLOTS)
        pad = small[0:C_HEADS * NEAR, 4352:4352 + SKEW]
        stage = small[0:2, 4608:5632].rearrange("p (s n) -> p s n", s=2)
        modrow = big[0:32, 9216:9216 + PARTS * P].rearrange("p (t n) -> p t n", t=PARTS)
        adab = big[0:32, 9216 + PARTS * P:9216 + 2 * PARTS * P].rearrange("p (t n) -> p t n", t=PARTS)
        lam_in = small[:, 4096:4096 + 4 * HD]
        keys = small[:, 0:2048].rearrange("p (t n) -> p t n", t=16)
        keysT = small[:, 2048:4096].rearrange("p (t n) -> p t n", t=16)
        work = small[:, 4096:4352].rearrange("p (s n) -> p s n", s=2)
        work2 = small[:, 4352:4608].rearrange("p (s n) -> p s n", s=2)
        cand = small[:, 4608:4864]
        cand2 = small[:, 4864:5120]
        onehot = small[:, 5120:5632]
        w_rows = [[ring_w[:, s, 2 * i:2 * i + 2, :].rearrange("p a b -> p (a b)") for i in range(4)]
                  for s in range(2)]
        uring = [mb[:, i // 2, i % 2, :] for i in range(RING0)] + w_rows[0]
        vring = [keys[:, 8 * i:8 * i + 8, :].rearrange("p t n -> p (t n)") for i in range(2)] + \
                [big[:, 15360 + 1024 * i:15360 + 1024 * (i + 1)] for i in range(2)] + w_rows[1]
        crow = small[0:16, 0:P]
        cth = small[0:16, P:2 * P]

        ident = sb("ident", [P, P])
        iota = sb("iota", [P, TOPK])
        rope_c = sb("rope_c", [P, LAT, HD])
        rope_s = sb("rope_s", [P, LAT, HD])
        win_mask = sb("win_mask", [P, GRID_W])
        gains = sb("gains", [P, 6, HD])
        subln = sb("subln", [P, 2 * HD])
        lam2 = sb("lam2", [P, 2])
        neg_lam = sb("neg_lam", [P, 1])
        cT = sb("cT", [P, 16])
        ss = sb("ss", [P, NCH])
        rstd = sb("rstd", [P, NCH])
        hss = sb("hss", [P, NCH * 16])
        hrs = sb("hrs", [P, NCH * 16])
        negmax = sb("negmax", [P, 64])
        rsum = sb("rsum", [P, 64])
        rinv = sb("rinv", [P, 16])
        oss = sb("oss", [P, NCH * B_HEADS])
        ors = sb("ors", [P, NCH * B_HEADS])
        top = sb("top", [P, 2, TOPK])
        topi = sb("topi", [P, 2, TOPK], U32)
        topif = sb("topif", [P, 2, TOPK])
        bpos = sb("bpos", [P, TOPK], U32)
        bij = sb("bij", [P, 2, TOPK], U32)
        bijf = sb("bijf", [P, 2, TOPK])
        seli = sb("seli", [P, 2, TOPK])
        best, expf, gexp, dots, coef = [sb(name, [P, TURN, TOPK]) for name in (
            "best",
            "expf",
            "gexp",
            "dots",
            "coef")]
        idxu = sb("idxu", [P, TURN, TOPK], U32)
        idxv = sb("idxv", [P, TURN, TOPK], U32)
        nbest = sb("nbest", [P, TURN])
        gsum = sb("gsum", [P, TURN])
        ginv = sb("ginv", [P, 1])
        gz = sb("gz", [P, TOPK])
        gz2 = sb("gz2", [P, TOPK])
        gth = sb("gth", [P, TOPK])
        ps = ctx.enter_context(nc.psum_tensor("ps", [P, 8, 512], F32))

        mod_dram = nc.dram_tensor("mod_scratch", [LAYERS, 2, 6 * D], F32, kind="Internal").ap()
        skew_dram = nc.dram_tensor("skew_scratch", [C_HEADS * NEAR, GRID_W, SKEW], F32, kind="Internal").ap()

        const_in = sem("const_in")
        c_in = sem("c_in")
        x_in = sem("x_in")
        adab_in = sem("adab_in")
        w_in = [sem(f"w_in{s}") for s in range(2)]
        mod_part = [sem(f"mod_part{s}") for s in range(2)]
        mod_out = [sem(f"mod_out{n}") for n in range(LAYERS)]
        mod01_in = [[sem(f"mod01_in{n}_{k}") for k in range(2)] for n in range(LAYERS)]
        mod2_in = [[sem(f"mod2_in{n}_{k}") for k in range(2)] for n in range(LAYERS)]
        pad_in = sem("pad_in")
        skew_out = sem("skew_out")
        bias_in = [sem(f"bias_in{s}") for s in range(BIAS_SLOTS)]
        keys_in = [sem(f"keys_in{n}") for n in range(LAYERS)]
        u_in = [sem(f"u_in{s}") for s in range(RING)]
        v_in = [sem(f"v_in{s}") for s in range(RING)]
        out_done = sem("out_done")
        w_free = [sem(f"w_free{s}") for s in range(2)]
        bank_free = [sem(f"bank_free{b}") for b in range(8)]
        mod01_free = sem("mod01_free")
        mod2_free = sem("mod2_free")
        bias_free = sem("bias_free")
        keys_free = sem("keys_free")
        w_rows_free = [sem(f"w_rows_free{s}") for s in range(2)]
        u_free = sem("u_free")
        v_free = sem("v_free")
        diag_free = sem("diag_free")
        modrow_rdy = sem("modrow_rdy")
        pad_rdy = sem("pad_rdy")
        silu_rdy = sem("silu_rdy")
        cs_rdy = sem("cs_rdy")
        cT_rdy = sem("cT_rdy")
        crT_rdy = sem("crT_rdy")
        ada_rdy = sem("ada_rdy")
        lam_rdy = sem("lam_rdy")
        lamx_rdy = sem("lamx_rdy")
        sq_in = sem("sq_in")
        sq_rdy = sem("sq_rdy")
        ss_rdy = sem("ss_rdy")
        x_rdy = sem("x_rdy")
        h_rdy = sem("h_rdy")
        tr_rdy = sem("tr_rdy")
        hT_rdy = sem("hT_rdy")
        proj_rdy = sem("proj_rdy")
        qkv_rdy = sem("qkv_rdy")
        qk_rdy = sem("qk_rdy")
        ka_rdy = sem("ka_rdy")
        last_rdy = sem("last_rdy")
        kdup_rdy = sem("kdup_rdy")
        qkT_rdy = sem("qkT_rdy")
        s_rdy = sem("s_rdy")
        max_rdy = sem("max_rdy")
        p_rdy = sem("p_rdy")
        pT_rdy = sem("pT_rdy")
        o_rdy = sem("o_rdy")
        on_rdy = sem("on_rdy")
        oT_rdy = sem("oT_rdy")
        op_rdy = sem("op_rdy")
        keysT_rdy = sem("keysT_rdy")
        qry_rdy = sem("qry_rdy")
        sc_rdy = sem("sc_rdy")
        score_rdy = sem("score_rdy")
        peer_go = sem("peer_go")
        idxu_rdy = sem("idxu_rdy")
        idxv_rdy = sem("idxv_rdy")
        best_rdy = sem("best_rdy")
        gexp_rdy = sem("gexp_rdy")
        gz_rdy = sem("gz_rdy")
        gth_rdy = sem("gth_rdy")
        coef_rdy = sem("coef_rdy")
        diag_rdy = sem("diag_rdy")
        y_rdy = sem("y_rdy")
        u_rows_done = sem("u_rows_done")
        layer_done = sem("layer_done")
        x_out_rdy = sem("x_out_rdy")
        own_v = sem("own_v")
        own_a = sem("own_a")
        own_t = sem("own_t")

        ADA_TILES = 6 * D // 512
        chunks_out = [NCH, LAT]
        groups = [n * HEADS for n in chunks_out]
        win = [a["ab_w_in"], a["c_w_in"]]
        wout = [a["ab_w_out"], a["c_w_out"]]
        in_width = [384, 512]
        IN_TILES = 6
        ADA_BANK = (4, 5)
        ADA_GAPS = {"a": (0, 2), "b": (2, 8), "out": (8, 10), "norm2": (10, 12)}
        W_FIRST = {(0, "ada"): 0, (0, "in"): 12, (1, "ada a"): 17, (1, "ada b"): 19, (0, "in last"): 25,
                   (1, "ada out"): 26, (0, "out"): 28, (1, "ada norm2"): 30, (0, "query"): 32,
                   (1, "in"): 36, (1, "in last"): 41, (1, "out"): 42, (1, "query"): 44}

        def w_slot(n, stage, t):
            return (W_FIRST[n, stage] + t) % 2

        def w_landed(n, stage, t):
            return 16 * ((W_FIRST[n, stage] + t) // 2 + 1)

        def qcol(n, c, col):
            if n == 0:
                return c * AB_IN + col
            return c * 3 * D + col if c < LAT else LAT * 3 * D + (c - LAT) * 2 * D + col - D

        def units(n):
            found = []
            if n == 0:
                for c in range(NCH):
                    for hh in range(A_HEADS):
                        found.append(dict(c=c, q=hh // 2, k=4 + hh // 4, half=hh % 2, v=A_V0 + HD * (hh // 4), w=HD,
                                          bank=0, col=hh * HD, bias=None, group=c, last=hh == A_HEADS - 1,
                                          first=hh == 0))
                for c in range(NCH):
                    for s in range(2 * B_HEADS):
                        found.append(dict(c=c, q=6 + s // 2, k=10 + s // 2, half=s % 2, v=B_V0 + 2 * HD * (s // 2),
                                          w=2 * HD, bank=s // 4, col=(s % 4) * 2 * HD, bias=None, group=NCH + c,
                                          last=s == 2 * B_HEADS - 1, first=s == 0))
            else:
                for hh in range(C_HEADS):
                    for c in range(LAT):
                        found.append(dict(c=c, q=hh // 2, k=8 + hh // 2, half=hh % 2, v=2 * D + HD * hh, w=HD,
                                          bank=c, col=(hh % 8) * HD, bias=hh, group=hh // 8,
                                          last=hh % 8 == 7 and c == 1, first=hh % 8 == 0 and c == 0))
            return found

        S_BANK = (4, 5, 7)
        PT_BANK = 6

        def row_slot(g, k):
            return k % RING0 if g < SMALL else (k + RING0) % RING

        def rows_landed(n, g, k):
            s = row_slot(g, k)
            small = SMALL * TOPK // RING0 if s < RING0 else 0
            before = sum(small + (G - SMALL) * TOPK // RING for G in groups[:n])
            if g < SMALL:
                return before + g * TOPK // RING0 + k // RING0 + 1
            return before + small + (g - SMALL) * TOPK // RING + k // RING + 1

        def group_banks(n, u):
            b0 = 2 * (u["group"] % 2)
            return (b0,) if n == 0 and u["w"] == HD else (b0, b0 + 1)

        def kT(n, u):
            c0 = 0 if u["c"] < LAT else LAT
            rows = slice(HD * u["half"], HD * u["half"] + HD)
            if n == 0:
                return qkT[rows, u["k"], c0 * P:NCH * P], c0
            t = u["k"] - 8
            return cT_k[rows, t, :], 0

        cT_q = big[:, QKT0:QKT0 + 8 * 256].rearrange("p (t n) -> p t n", t=8)
        cT_k = big[:, QKT0 + 2048:QKT0 + 2048 + 8 * 512].rearrange("p (t n) -> p t n", t=8)

        def qT(n, u):
            rows = slice(HD * u["half"], HD * u["half"] + HD)
            cols = slice(u["c"] * P, u["c"] * P + P)
            return qkT[rows, u["q"], cols] if n == 0 else cT_q[rows, u["q"], cols]

        def spread(vec, n):
            return bass.AP(tensor=vec.tensor, offset=vec.offset, ap=[[0, P], [1, n]])

        block = ctx.enter_context(nc.Block())

        @block.sync
        def _(sp):
            sp.dma_start(crow[0:8, :], a["c"].rearrange("a (k p) -> (a k) p", p=P)).then_inc(c_in, 16)
            sp.dma_start(crow[8:16, :], a["c_ctx"].rearrange("(k p) -> k p", p=P)).then_inc(c_in, 16)
            sp.dma_start(ident[:], a["ident"]).then_inc(c_in, 16)
            consts = [(iota, a["iota"]), (win_mask, a["win_mask"]),
                      (rope_c, a["rope_c"].rearrange("(c p) n -> p c n", p=P)),
                      (rope_s, a["rope_s"].rearrange("(c p) n -> p c n", p=P))]

            def load_adab(n):
                for s in range(2):
                    sp.dma_start(adab[16 * s:16 * s + 16, :, :], a["ada_b"][n].rearrange("(t j p) -> j t p", t=PARTS, p=P))\
                      .then_inc(adab_in, 16)

            def load_tile(slot, src, width):
                take(sp, w_free[slot])
                sp.dma_start(ring_w[:, slot, :, 0:width], src).then_inc(w_in[slot], 16)

            def load_ada(n, first, last, slot0=0):
                src = a["ada_w"][n].rearrange("(k p) m -> p k m", p=P)
                with sp.Fori(0, (last - first) // 2) as i:
                    for j in range(2):
                        load_tile((slot0 + j) % 2, src[:, :, bass.ds(i * 1024 + (first + j) * 512, 512)], 512)

            ada0 = a["ada_w"][0].rearrange("(k p) m -> p k m", p=P)
            load_ada(0, 0, 2)
            for dst, src in consts:
                sp.dma_start(dst[:], src).then_inc(const_in, 16)
            load_adab(0)
            sp.dma_start(xs[:, 0:LAT, :], a["x"][0].rearrange("(c p) n -> p c n", p=P)).then_inc(x_in, 16)
            sp.dma_start(xs[:, LAT:NCH, :], a["ctx"][0].rearrange("(c p) n -> p c n", p=P)).then_inc(x_in, 16)
            load_ada(0, 2, 6)
            small_in = [(gains[:, k, :], a[name][0]) for k, name in enumerate(
                ["a_q_norm", "a_k_norm", "b_q_norm", "b_k_norm", "c_q_norm", "c_k_norm"])]
            for dst, src in small_in:
                sp.dma_start(dst, spread(src, HD)).then_inc(const_in, 16)
            sp.dma_start(subln[:], spread(a["b_subln"], 2 * HD)).then_inc(const_in, 16)
            sp.dma_start(lam_in, spread(a["b_lambda"], 4 * HD)).then_inc(const_in, 16)

            def mod_to_dram(n, part):
                take(sp, modrow_rdy)
                for s in range(2):
                    sp.dma_start(mod_dram[n, s, part * 2 * D:(part + 1) * 2 * D].rearrange("(j p) -> j p", p=P),
                                 modrow[16 * s:16 * s + 16, part, :]).then_inc(mod_out[n], 16)
                sp.wait_ge(mod_out[n], 32 * (part + 1))

            def load_mod(n, first, rows, slot, done):
                for s in range(2):
                    src = mod_dram[n, s, first * D:(first + rows) * D]
                    sp.dma_start(mb[:, s, slot:slot + rows, :].rearrange("p r n -> p (r n)"),
                                 spread(src, rows * D)).then_inc(done, 16)

            def load_bias(first, last):
                for hh in range(first, last):
                    take(sp, bias_free)
                    for odd in range(2):
                        src = bass.AP(tensor=skew_dram.tensor,
                                      offset=(hh * NEAR + 1 - odd) * GRID_W * SKEW + GRID_W - 1,
                                      ap=[[SKEW - 1, GRID_W], [GRID_W * SKEW, 6], [1, GRID_W]])
                        dst = bias[GRID_W * odd:GRID_W * odd + GRID_W, hh % BIAS_SLOTS, :]
                        sp.dma_start(dst.rearrange("p (i c) -> p i c", i=6), src)\
                          .then_inc(bias_in[hh % BIAS_SLOTS], 16)

            for n in range(LAYERS):
                wi = win[n][0].rearrange("(k p) m -> p k m", p=P)
                width = in_width[n]
                if n == 1:
                    take(sp, u_rows_done)
                sp.dma_start(grow[:], spread(a["norm_g"][n, 0], D)).then_inc(mod01_in[n][0], 16)
                if n == 0:
                    load_tile(0, ada0[:, :, 6 * 512:7 * 512], 512)
                    mod_to_dram(0, 0)
                    load_tile(1, ada0[:, :, 7 * 512:8 * 512], 512)
                load_mod(n, 0, 2, 0, mod01_in[n][0])
                if n == 0:
                    load_ada(0, 8, ADA_TILES)
                    for slot in range(2):
                        load_tile(slot, wi[:, :, slot * width:(slot + 1) * width], width)
                    mod_to_dram(0, 1)
                if n == 1:
                    for slot in range(2):
                        load_tile(slot, wi[:, :, slot * width:(slot + 1) * width], width)
                    take(sp, layer_done)
                load_mod(n, 2, 1, 2, mod2_in[n][0])
                if n == 0:
                    mod_to_dram(0, 2)
                    load_adab(1)
                take(sp, mod01_free)
                sp.dma_start(grow[:], spread(a["norm_g"][n, 1], D)).then_inc(mod01_in[n][1], 16)
                load_mod(n, 3, 2, 0, mod01_in[n][1])
                if n == 1:
                    load_bias(0, BIAS_SLOTS)
                for t in range(2, IN_TILES - 1):
                    load_tile(w_slot(n, "in", t), wi[:, :, t * width:(t + 1) * width], width)
                if n == 0:
                    take(sp, pad_rdy)
                    sp.dma_start(pad[:, 48:48 + 31], a["rpb_near"]).then_inc(pad_in, 16)
                    sp.wait_ge(pad_in, 16)
                    sp.dma_start(skew_dram, bass.AP(tensor=pad.tensor, offset=pad.offset,
                                                    ap=[list(pad.ap[0]), [0, GRID_W], [1, SKEW]]))\
                      .then_inc(skew_out, 16)
                    load_ada(1, 0, ADA_GAPS["b"][1], w_slot(1, "ada a", 0))
                load_tile(w_slot(n, "in last", 0), wi[:, :, (IN_TILES - 1) * width:IN_TILES * width], width)
                if n == 0:
                    load_ada(1, *ADA_GAPS["out"])
                    mod_to_dram(1, 0)
                    mod_to_dram(1, 1)
                wo = wout[n][0].rearrange("(k p) m -> p k m", p=P)
                for slot in range(2):
                    load_tile(slot, wo[:, :, slot * 512:(slot + 1) * 512], 512)
                if n == 1:
                    load_bias(BIAS_SLOTS, C_HEADS)
                take(sp, keys_free)
                sp.dma_start(keys, a["peer_keys"][n].rearrange("h q n d -> n (h q) d")).then_inc(keys_in[n], 16)
                if n == 0:
                    load_ada(1, *ADA_GAPS["norm2"])
                wq = a["peer_w_q"][n].rearrange("(k p) m -> p k m", p=P)
                for slot in range(2):
                    load_tile(slot, wq[:, :, slot * 512:(slot + 1) * 512], 512)
                take(sp, mod2_free)
                load_mod(n, 5, 1, 2, mod2_in[n][1])
                if n == 0:
                    mod_to_dram(1, 2)
                for slot in range(2):
                    load_tile(slot, wq[:, :, (2 + slot) * 512:(3 + slot) * 512], 512)
                if n == 0:
                    sp.wait_ge(skew_out, 16)
            take(sp, x_out_rdy)
            sp.dma_start(out[0].rearrange("(c p) n -> p c n", p=P), xs[:, 0:LAT, :]).then_inc(out_done, 16)
            sp.wait_ge(out_done, 16)

        @block.gpsimd
        def _(pool):
            def gather(table, idx, row, room, landed):
                take(pool, room)
                pool.indirect_dma_start(row, None, table, bass.IndirectOffsetOnAxis(idx, 0)).then_inc(landed, 16)

            def step(n, g, u=True, v=True):
                if u:
                    take(pool, idxu_rdy)
                if v:
                    take(pool, idxv_rdy)
                for k in range(TOPK):
                    if u:
                        s = row_slot(g, k)
                        gather(a[f"peer_u{n}"], idxu[:, g % TURN, k:k + 1], uring[s], u_free, u_in[s])
                    if v:
                        s = row_slot(g - LAG, k)
                        gather(a[f"peer_v{n}"], idxv[:, (g - LAG) % TURN, k:k + 1], vring[s], v_free, v_in[s])

            for n in range(LAYERS):
                G = groups[n]
                take(pool, peer_go)
                pool.sem_inc(u_free, RING0)
                pool.sem_inc(v_free, RING0)
                for g in range(LAG):
                    step(n, g, v=False)
                take(pool, w_rows_free[0])
                pool.sem_inc(u_free, RING - RING0)
                for g in range(LAG, TURN):
                    step(n, g)
                take(pool, w_rows_free[1])
                pool.sem_inc(v_free, RING - RING0)
                with pool.Fori(0, G // TURN - 1):
                    for j in range(TURN):
                        step(n, TURN + j)
                for g in range(G, G + LAG):
                    step(n, g, u=False)
                    if g == G:
                        take(pool, u_free, RING)
                        pool.sem_inc(w_free[0], 1)
                take(pool, v_free, RING)
                pool.sem_inc(w_free[1], 1)

        @block.scalar
        def _(act):
            bank = [0]
            own = Chain(act, own_a)

            def copy(dst, src):
                return nc.scalar.activation(dst, src, ACT.Copy)

            def tr_out(dst, width=512, shape=None):
                b = 6 + bank[0] % 2
                bank[0] += 1
                take(act, tr_rdy)
                src = ps[:, b, 0:width]
                if shape:
                    src = src.rearrange("p (t n) -> p t n", t=shape)
                copy(dst, src).then_inc(bank_free[b], 1)

            def rows_out(chunks, rdy):
                for c in chunks:
                    for half in range(2):
                        tr_out(hT[:, 4 * half:4 * half + 4, c * P:(c + 1) * P], shape=4)
                act.drain().then_inc(rdy, 1)

            def sumsq(c0, c1):
                for c in range(c0, c1):
                    nc.scalar.activation(h[:, c, :], xs[:, c, :], ACT.Square, accum_out=ss[:, c:c + 1])\
                      .then_inc(ss_rdy, 1)

            def root(t):
                take(act, sq_in)
                nc.scalar.activation(t, t, ACT.Sqrt).then_inc(sq_rdy, 1)

            def ada_out(n, t, part, turns=0):
                slot, T = t % 2, n * ADA_TILES + t
                if T >= 2:
                    act.wait_ge(mod_part[slot], turns + 32 * (T // 2))
                take(act, ada_rdy)
                own.add(copy(stage[:, slot, :], ps[0:2, ADA_BANK[slot], :]))
                own.wait()
                act.sem_inc(bank_free[ADA_BANK[slot]], 1)
                for s in range(2):
                    p0 = 16 * s + 4 * (t % 4)
                    act.dma_start(modrow[p0:p0 + 4, part, :], stage[s:s + 1, slot, :].rearrange("s (j p) -> s j p", p=P))\
                       .then_inc(mod_part[slot], 16)

            def ada_outs(gap):
                for t in range(*ADA_GAPS[gap]):
                    if t == 0:
                        act.wait_ge(mod_out[0], 32 * PARTS)
                    ada_out(1, t, t // 4)

            def norm_sums(c0, c1):
                for c in range(c0, c1):
                    take(act, x_rdy)
                    sumsq(c, c + 1)
                root(ss[:, c0:c1])

            act.wait_ge(c_in, 48)
            nc.scalar.activation(cth[:], crow[:], ACT.Tanh, scale=0.5).then_inc(silu_rdy, 1)
            for t in range(2):
                ada_out(0, t, 0)
            for n in range(LAYERS):
                co = chunks_out[n]
                if n == 0:
                    act.wait_ge(x_in, 32)
                    sumsq(0, NCH)
                    root(ss[:])
                    for t in range(2, 4):
                        ada_out(0, t, 0)
                else:
                    rows_out(range(NCH - 1), hT_rdy)
                    norm_sums(NCH - 1, NCH)
                if n == 0:
                    own.reset()
                    with act.Fori(0, PARTS - 1) as i:
                        for j in range(4):
                            ada_out(0, 4 + j, i + 1, i * 64)
                        own.reset()
                    rows_out(range(NCH), hT_rdy)
                if n == 0:
                    take(act, lam_rdy)
                    nc.scalar.activation(lam2[:], lam2[:], ACT.Exp).then_inc(lamx_rdy, 1)
                width = in_width[n]
                first = NCH if n == 0 else LAT
                def proj_out(t, c):
                    take(act, proj_rdy)
                    q0 = qcol(n, c, t * width)
                    copy(big[:, q0:q0 + width], ps[:, c, 0:width]).then_inc(bank_free[c], 1)

                for t in range(2):
                    for c in range(first):
                        proj_out(t, c)
                act.drain().then_inc(qkv_rdy, 1)
                if n == 1:
                    rows_out([NCH - 1], hT_rdy)
                root(hss[:, 0:first * (10 if n == 0 else 16)])
                for t in range(2, IN_TILES - 1):
                    if t == 4 and n == 1:
                        act.drain().then_inc(qkv_rdy, 1)
                    for c in range(NCH):
                        if t == 4 and n == 1 and c == 2:
                            root(hss[:, 0:NCH * 16])
                        proj_out(t, c)
                if n == 0:
                    act.drain().then_inc(qkv_rdy, 1)
                if n == 0:
                    ada_outs("a")
                    take(act, ka_rdy)
                    for c in range(NCH):
                        q0 = qcol(0, c, A_K0)
                        src = big[:, q0:q0 + 2 * HD]
                        src = bass.AP(tensor=src.tensor, offset=src.offset,
                                      ap=[list(src.ap[0]), [HD, 2], [0, 2], [1, HD]])
                        copy(kdup[:, c, :].rearrange("p (a b n) -> p a b n", a=2, b=2), src)
                    act.drain().then_inc(kdup_rdy, 1)
                if n == 0:
                    for t in range(6):
                        tr_out(qkT[:, t, :])
                    root(hss[:, 0:NCH * 16])
                    ada_outs("b")
                    for t in range(6, 14):
                        tr_out(qkT[:, t, :])
                else:
                    for t in range(8):
                        tr_out(cT_q[:, t, :], width=256)
                    for t in range(8):
                        tr_out(cT_k[:, t, :])
                act.drain().then_inc(qkT_rdy, 1)
                us = units(n)

                def exp(u):
                    nk = (NCH if us[u]["c"] < LAT else NCH - LAT) * P
                    take(act, max_rdy)
                    nc.scalar.activation(prob[:, u % 2, 0:nk], ps[:, S_BANK[u % 3], 0:nk], ACT.Exp,
                                         bias=negmax[:, u:u + 1], accum_out=rsum[:, u:u + 1]).then_inc(p_rdy, 1)

                def pT_out(u):
                    nk = (NCH if us[u]["c"] < LAT else NCH - LAT) * P
                    take(act, tr_rdy)
                    copy(probT[:, u % 2, 0:nk], ps[:, PT_BANK, 0:nk]).then_inc(pT_rdy, 1)

                for c in range(NCH - 1):
                    proj_out(IN_TILES - 1, c)
                exp(0)
                proj_out(IN_TILES - 1, NCH - 1)
                act.drain().then_inc(last_rdy, 1)
                for u in range(len(us)):
                    if u + 1 < len(us):
                        exp(u + 1)
                    pT_out(u)
                if n == 0:
                    root(oss[:])
                    ada_outs("out")
                rows_out(range(co), oT_rdy)
                for t in range(4):
                    tr_out(keysT[:, 4 * t:4 * t + 4, :].rearrange("p t n -> p (t n)"))
                act.drain().then_inc(keysT_rdy, 1)
                for c in range(co - 1):
                    norm_sums(c, c + 1)
                rows_out(range(co - 1), hT_rdy)
                norm_sums(co - 1, co)
                if n == 0:
                    ada_outs("norm2")
                rows_out([co - 1], hT_rdy)

                def query_out(t):
                    for j in range(4):
                        take(act, proj_rdy)
                        copy(qryT[:, j, 0:co * P], ps[:, 2 + j, 0:co * P]).then_inc(bank_free[2 + j], 1)
                    act.drain().then_inc(qry_rdy, 1)
                    for c in range(co):
                        take(act, sc_rdy)
                        s0 = (t * co + c) * 512
                        copy(scores[:, s0:s0 + 512], ps[:, 6 + c % 2, :]).then_inc(bank_free[6 + c % 2], 1)
                    act.drain().then_inc(score_rdy, 1)

                def weights_exp(g):
                    b = g % TURN
                    take(act, best_rdy)
                    nc.scalar.activation(gexp[:, b, :], best[:, b, :], ACT.Exp, bias=nbest[:, b:b + 1],
                                         accum_out=gsum[:, b:b + 1]).then_inc(gexp_rdy, 1)

                def diagonals(g):
                    take(act, coef_rdy)
                    for k in range(TOPK):
                        take(act, diag_free)
                        nc.scalar.activation(diag[:, k % DIAGS, :], ident[:], ACT.Copy,
                                             scale=coef[:, g % TURN, k:k + 1]).then_inc(diag_rdy, 1)

                def step(g, topk=True, u=True, v=True):
                    if v:
                        diagonals(g - LAG)
                    if topk:
                        weights_exp(g + 1)
                    if u:
                        take(act, gz_rdy)
                        nc.scalar.activation(gth[:], gz[:], ACT.Tanh, scale=GELU_C).then_inc(gth_rdy, 1)

                G = groups[n]
                if n == 0:
                    act.sem_inc(diag_free, DIAGS - 1)
                query_out(0)
                weights_exp(0)
                for g in range(LAG):
                    query_out(1 + g)
                    step(g, v=False)
                query_out(3)
                for g in range(LAG, TURN):
                    step(g)
                with act.Fori(0, G // TURN - 2):
                    for j in range(TURN):
                        step(TURN + j)
                for g in range(G - TURN, G + LAG):
                    step(g, topk=g < G - 1, u=g < G)
                if n == 0:
                    norm_sums(0, NCH - 1)

        @block.tensor
        def _(pe):
            bank = [0]
            for b in range(8):
                pe.sem_inc(bank_free[b], 1)
            for s in range(2):
                pe.sem_inc(w_free[s], 1)

            def transposes(srcs):
                b = 6 + bank[0] % 2
                bank[0] += 1
                take(pe, bank_free[b])
                for j, src in enumerate(srcs):
                    mm = nc.tensor.transpose(ps[:, b, j * P:(j + 1) * P], src, ident[:])
                mm.then_inc(tr_rdy, 1)

            def rows(src, chunks, rdy):
                for c in chunks:
                    take(pe, rdy)
                    for half in range(2):
                        transposes([src[:, c, (4 * half + j) * P:(4 * half + j + 1) * P] for j in range(4)])

            def project(slot, chunks, width, done):
                for c in chunks:
                    take(pe, bank_free[c])
                    for k in range(KD):
                        mm = nc.tensor.matmul(ps[:, c, 0:width], hT[:, k, c * P:(c + 1) * P],
                                              ring_w[:, slot, k, 0:width], start=(k == 0), stop=(k == KD - 1))
                    mm.then_inc(done, 1)
                pe.drain().then_inc(w_free[slot], 1)

            take(pe, cs_rdy)
            pe.wait_ge(c_in, 48)
            take(pe, bank_free[4])
            nc.tensor.transpose(ps[:, 4, 0:16], crow[:], ident[0:16, 0:16]).then_inc(crT_rdy, 1)
            take(pe, cT_rdy)

            def ada_tile(slot, t):
                b = ADA_BANK[t % 2]
                take(pe, bank_free[b])
                for k in range(KD):
                    mm = nc.tensor.matmul(ps[0:2, b, :], cT[:, k:16:8], ring_w[:, slot, k, :],
                                          start=(k == 0), stop=(k == KD - 1))
                mm.then_inc(ada_rdy, 1)
                pe.drain().then_inc(w_free[slot], 1)

            def ada_gap(gap):
                for t in range(*ADA_GAPS[gap]):
                    at = 1, "ada " + gap, t - ADA_GAPS[gap][0]
                    pe.wait_ge(w_in[w_slot(*at)], w_landed(*at))
                    ada_tile(w_slot(*at), t)

            with pe.Fori(0, ADA_TILES // 2) as i:
                for slot in range(2):
                    pe.wait_ge(w_in[slot], i * 16 + 16)
                    ada_tile(slot, slot)
            for n in range(LAYERS):
                co = chunks_out[n]
                rows(h, range(NCH if n == 0 else NCH - 1), h_rdy)
                take(pe, hT_rdy)
                width = in_width[n]
                for t in range(IN_TILES - 1):
                    if n == 1 and t == 2:
                        rows(h, [NCH - 1], h_rdy)
                        take(pe, hT_rdy)
                    slot = w_slot(n, "in", t)
                    pe.wait_ge(w_in[slot], w_landed(n, "in", t))
                    project(slot, range(LAT if n == 1 and t < 2 else NCH), width, proj_rdy)
                if n == 0:
                    ada_gap("a")
                take(pe, qk_rdy)
                if n == 0:
                    for t in range(4):
                        transposes([big[:, qcol(0, c, t * P):qcol(0, c, t * P) + P] for c in range(NCH)])
                    take(pe, kdup_rdy)
                    for t in range(2):
                        transposes([kdup[:, c, t * P:(t + 1) * P] for c in range(NCH)])
                    ada_gap("b")
                    take(pe, qk_rdy)
                    for t in range(8):
                        transposes([big[:, qcol(0, c, B_Q0 + t * P):qcol(0, c, B_Q0 + t * P) + P] for c in range(NCH)])
                else:
                    for t in range(8):
                        transposes([big[:, qcol(1, c, t * P):qcol(1, c, t * P) + P] for c in range(LAT)])
                    take(pe, qk_rdy)
                    for t in range(8):
                        transposes([big[:, qcol(1, c, D + t * P):qcol(1, c, D + t * P) + P] for c in range(NCH)])
                take(pe, qkT_rdy)
                us = units(n)
                for b in range(4, 8):
                    take(pe, bank_free[b])

                def score(u):
                    keyT, c0 = kT(n, us[u])
                    nc.tensor.matmul(ps[:, S_BANK[u % 3], 0:(NCH - c0) * P], qT(n, us[u]), keyT, start=True, stop=True)\
                        .then_inc(s_rdy, 1)

                def prob_T(u):
                    take(pe, p_rdy)
                    if u:
                        take(pe, pT_rdy)
                    for j in range(NCH if us[u]["c"] < LAT else NCH - LAT):
                        mm = nc.tensor.transpose(ps[:, PT_BANK, j * P:(j + 1) * P],
                                                 prob[:, u % 2, j * P:(j + 1) * P], ident[:])
                    mm.then_inc(tr_rdy, 1)

                def values(u):
                    q = us[u]
                    b0 = 2 * (q["group"] % 2)
                    if u == 0:
                        take(pe, last_rdy)
                    if q["first"]:
                        for b in group_banks(n, q):
                            take(pe, bank_free[b])
                    c0 = 0 if q["c"] < LAT else LAT
                    for j in range(NCH - c0):
                        v0 = qcol(n, c0 + j, q["v"])
                        mm = nc.tensor.matmul(ps[:, b0 + q["bank"], q["col"]:q["col"] + q["w"]],
                                              probT[:, u % 2, j * P:(j + 1) * P], big[:, v0:v0 + q["w"]],
                                              start=(j == 0), stop=(c0 + j == NCH - 1))
                    if q["last"]:
                        mm.then_inc(o_rdy, 1)

                for u in range(2):
                    score(u)
                slot = w_slot(n, "in last", 0)
                pe.wait_ge(w_in[slot], w_landed(n, "in last", 0))
                project(slot, range(NCH), width, proj_rdy)
                for u in range(len(us)):
                    if u + 2 < len(us):
                        score(u + 2)
                    prob_T(u)
                    if u:
                        values(u - 1)
                take(pe, pT_rdy)
                values(len(us) - 1)
                pe.drain().then_inc(own_t, 1)
                pe.wait_ge(own_t, n + 1)
                for b in range(4, 8):
                    pe.sem_inc(bank_free[b], 1)
                bank[0] = 0
                if n == 0:
                    ada_gap("out")
                rows(o, range(co), on_rdy)
                take(pe, oT_rdy)
                for slot in range(2):
                    if slot == 1:
                        pe.wait_ge(keys_in[n], 16)
                        for t in range(4):
                            transposes([keys[:, 4 * t + j, :] for j in range(4)])
                    pe.wait_ge(w_in[slot], w_landed(n, "out", slot))
                    project(slot, range(co), 512, op_rdy)
                rows(h, range(co - 1), h_rdy)
                if n == 0:
                    ada_gap("norm2")
                rows(h, [co - 1], h_rdy)
                take(pe, hT_rdy, 2)
                take(pe, keysT_rdy)
                for t in range(4):
                    slot = t % 2
                    pe.wait_ge(w_in[slot], w_landed(n, "query", t))
                    for j in range(4):
                        take(pe, bank_free[2 + j])
                        for k in range(KD):
                            mm = nc.tensor.matmul(ps[:, 2 + j, 0:co * P], ring_w[:, slot, k, j * P:(j + 1) * P],
                                                  hT[:, k, 0:co * P], start=(k == 0), stop=(k == KD - 1))
                        mm.then_inc(proj_rdy, 1)
                    pe.drain().then_inc(w_free[slot] if t < 2 else w_rows_free[slot], 1)
                    take(pe, qry_rdy)
                    for c in range(co):
                        take(pe, bank_free[6 + c % 2])
                        for j in range(4):
                            mm = nc.tensor.matmul(ps[:, 6 + c % 2, j * P:(j + 1) * P],
                                                  qryT[:, j, c * P:(c + 1) * P], keysT[:, 4 * t + j, :],
                                                  start=True, stop=True)
                        mm.then_inc(sc_rdy, 1)

                def expert_sum(g, later=0):
                    for b in range(2):
                        take(pe, bank_free[b])
                    for k in range(TOPK):
                        row = vring[row_slot(g, k)]
                        take(pe, diag_rdy)
                        pe.wait_ge(v_in[row_slot(g, k)], later + 16 * rows_landed(n, g, k))
                        nc.tensor.matmul(ps[:, 0, :], diag[:, k % DIAGS, :], row[:, 0:512],
                                         start=(k == 0), stop=(k == TOPK - 1)).then_inc(diag_free, 1)
                        nc.tensor.matmul(ps[:, 1, :], diag[:, k % DIAGS, :], row[:, 512:1024],
                                         start=(k == 0), stop=(k == TOPK - 1)).then_inc(v_free, 1)
                    pe.drain().then_inc(y_rdy, 1)

                for g in range(SMALL):
                    expert_sum(g)
                with pe.Fori(0, (groups[n] - SMALL) // 2) as i:
                    for j in range(2):
                        expert_sum(SMALL + j, i * (2 * 16 * TOPK // RING))

        @block.vector
        def _(dve):
            v = nc.vector
            own = Chain(dve, own_v)
            TT, STT, TS = v.tensor_tensor, v.scalar_tensor_tensor, v.tensor_scalar

            take(dve, silu_rdy)
            own.link(STT(crow, cth, 1.0, crow, ALU.add, ALU.mult))
            TS(crow, crow, 0.5, None, ALU.mult).then_inc(cs_rdy, 1)
            take(dve, crT_rdy)
            own.link(v.tensor_copy(cT[:], ps[:, 4, 0:16]))
            dve.sem_inc(cT_rdy, 1)
            dve.sem_inc(bank_free[4], 1)

            def mod_rows_out(n, part):
                for slot in range(2):
                    dve.wait_ge(mod_part[slot], 32 * (n * ADA_TILES // 2 + 2 * (part + 1)))
                dve.wait_ge(adab_in, 32 * (n + 1))
                own.link(TT(modrow[:, part, :], modrow[:, part, :], adab[:, part, :], ALU.add))
                dve.sem_inc(modrow_rdy, 1)

            def rms(sums, result, count, wait_ready=None):
                own.link(TS(sums, sums, 1.0 / count, EPS, ALU.mult, ALU.add))
                dve.sem_inc(sq_in, 1)
                take(dve, sq_rdy)
                own.link(v.reciprocal(result, sums))

            def mod_gain(loaded):
                dve.wait_ge(loaded, 16 * 3)
                for s in range(2):
                    own.link(STT(mb[:, s, 1, :], mb[:, s, 1, :], 1.0, grow[:], ALU.add, ALU.mult))

            def norm_root(c0, c1):
                take(dve, ss_rdy, c1 - c0)
                rms(ss[:, c0:c1], rstd[:, c0:c1], D)

            def norm_rows(c0, c1):
                for c in range(c0, c1):
                    s = 0 if c < LAT else 1
                    own.link(STT(h[:, c, :], xs[:, c, :], rstd[:, c:c + 1], mb[:, s, 1, :], ALU.mult, ALU.mult))
                    own.link(TT(h[:, c, :], h[:, c, :], mb[:, s, 0, :], ALU.add))
                    dve.sem_inc(h_rdy, 1)

            def head_sums(n, chunks, col, heads):
                for c in range(chunks):
                    q0 = qcol(n, c, col)
                    x = big[:, q0:q0 + heads * HD]
                    own.link(TT(tmpA[:, 0:heads * HD], x, x, ALU.mult))
                    own.link(v.tensor_reduce(hss[:, c * heads:(c + 1) * heads],
                                             tmpA[:, 0:heads * HD].rearrange("p (h n) -> p h n", n=HD), AX_X, ALU.add))

            def head_scale(n, chunks, col, heads, gain_of):
                for c in range(chunks):
                    q0 = qcol(n, c, col)
                    x = big[:, q0:q0 + heads * HD].rearrange("p (h n) -> p h n", n=HD)
                    r = hrs[:, c * heads:(c + 1) * heads].unsqueeze(2).to_broadcast([P, heads, HD])
                    own.link(TT(x, x, r, ALU.mult))
                    for h0, h1, g in gain_of:
                        own.add(TT(x[:, h0:h1, :], x[:, h0:h1, :],
                                   gains[:, g, :].unsqueeze(1).to_broadcast([P, h1 - h0, HD]), ALU.mult))
                    own.wait()
                    if n == 0 and c < LAT:
                        t1 = tmpA[:, 0:heads * HD].rearrange("p (h n) -> p h n", n=HD)
                        own.add(TT(t1, x, rope_c[:, c, :].unsqueeze(1).to_broadcast([P, heads, HD]), ALU.mult))
                        xv = x.rearrange("p h (x f i) -> p h x f i", x=2, f=2)
                        tv = tmpB[:, 0:heads * HD].rearrange("p (h x f i) -> p h x f i", x=2, f=2, i=16)
                        sv = rope_s[:, c, :].rearrange("p (x f i) -> p x f i", x=2, f=2)
                        for f in range(2):
                            own.add(TT(tv[:, :, :, f, :], xv[:, :, :, 1 - f, :],
                                       sv[:, :, f, :].unsqueeze(1).to_broadcast([P, heads, 2, 16]), ALU.mult))
                        own.wait()
                        own.link(TT(x, t1, tmpB[:, 0:heads * HD].rearrange("p (h n) -> p h n", n=HD), ALU.add))

            dve.wait_ge(x_in, 32)
            for n in range(LAYERS):
                co = chunks_out[n]
                if n == 0:
                    norm_root(0, NCH)
                    mod_rows_out(0, 0)
                    mod_gain(mod01_in[0][0])
                    norm_rows(0, NCH)
                else:
                    dve.sem_inc(bias_free, BIAS_SLOTS)
                    norm_root(NCH - 1, NCH)
                    norm_rows(NCH - 1, NCH)
                dve.sem_inc(mod01_free, 1)
                if n == 0:
                    mod_rows_out(0, 1)
                    mod_rows_out(0, 2)
                    own.link(v.memset(pad, 0.0))
                    dve.sem_inc(pad_rdy, 1)
                    dve.wait_ge(const_in, 16 * 12)
                    lv = lam_in.rearrange("p (a b n) -> p a b n", a=2, b=2)
                    own.link(TT(lv[:, :, 0, :], lv[:, :, 0, :], lv[:, :, 1, :], ALU.mult))
                    v.tensor_reduce(lam2[:], lv[:, :, 0, :], AX_X, ALU.add).then_inc(lam_rdy, 1)
                    take(dve, lamx_rdy)
                    own.link(TT(neg_lam[:], lam2[:, 1:2], lam2[:, 0:1], ALU.subtract))
                    own.link(TS(neg_lam[:], neg_lam[:], -LAM_INIT, None, ALU.add))
                    for g in (0, 2, 4):
                        own.link(TS(gains[:, g, :], gains[:, g, :], HD ** -0.5, None, ALU.mult))
                    own.link(TS(subln[:], subln[:], 1.0 - LAM_INIT, None, ALU.mult))

                take(dve, qkv_rdy)
                if n == 0:
                    head_sums(0, NCH, 0, 10)
                    rms(hss[:, 0:40], hrs[:, 0:40], HD)
                    head_scale(0, NCH, 0, 10, [(0, 8, 0), (8, 10, 1)])
                    dve.sem_inc(qk_rdy, 1)
                    dve.sem_inc(ka_rdy, 1)
                    take(dve, qkv_rdy)
                    head_sums(0, NCH, B_Q0, 16)
                    rms(hss[:], hrs[:], HD)
                    head_scale(0, NCH, B_Q0, 16, [(0, 8, 2), (8, 16, 3)])
                    dve.sem_inc(qk_rdy, 1)
                else:
                    head_sums(1, LAT, 0, 16)
                    rms(hss[:, 0:32], hrs[:, 0:32], HD)
                    head_scale(1, LAT, 0, 16, [(0, 16, 4)])
                    dve.sem_inc(qk_rdy, 1)
                    take(dve, qkv_rdy)
                    head_sums(1, NCH, D, 16)
                    rms(hss[:], hrs[:], HD)
                    head_scale(1, NCH, D, 16, [(0, 16, 5)])
                    dve.sem_inc(qk_rdy, 1)
                us = units(n)

                def row_max(u):
                    q = us[u]
                    nk = (NCH if q["c"] < LAT else NCH - LAT) * P
                    s = ps[:, S_BANK[u % 3], 0:nk]
                    if q["bias"] is not None:
                        b = bias[:, q["bias"] % BIAS_SLOTS, :]
                        if q["c"] == 0:
                            dve.wait_ge(bias_in[q["bias"] % BIAS_SLOTS], 32 * (q["bias"] // BIAS_SLOTS + 1))
                            b3 = b.rearrange("p (i c) -> p i c", i=6)
                            own.link(TT(b3, b3, win_mask[:].unsqueeze(1).to_broadcast([P, 6, GRID_W]), ALU.add))
                    take(dve, s_rdy)
                    if q["bias"] is not None:
                        first = (2 - 2 * q["c"]) * GRID_W
                        own.link(TT(s[:, 0:SEQ], s[:, 0:SEQ], b[:, first:first + SEQ], ALU.add))
                        if q["c"] == LAT - 1 and q["bias"] + BIAS_SLOTS < C_HEADS:
                            dve.sem_inc(bias_free, 1)
                    v.tensor_reduce(negmax[:, u:u + 1], s, AX_X, ALU.max, negate=True).then_inc(max_rdy, 1)

                def group_out(last):
                    q = us[last]
                    b0 = 2 * (q["group"] % 2)
                    take(dve, o_rdy)
                    if n == 0:
                        c = q["c"]
                        own.link(v.reciprocal(rinv[:, 0:8], rsum[:, last - 7:last + 1]))
                        if q["group"] < NCH:
                            own.link(TT(o[:, c, 0:512].rearrange("p (h n) -> p h n", n=HD),
                                        ps[:, b0, :].rearrange("p (h n) -> p h n", n=HD),
                                        rinv[:, 0:8].unsqueeze(2).to_broadcast([P, 8, HD]), ALU.mult))
                        else:
                            t = tmpA.rearrange("p (s n) -> p s n", n=2 * HD)
                            own.link(TT(t, ps[:, b0:b0 + 2, :].rearrange("p b (s n) -> p (b s) n", n=2 * HD),
                                        rinv[:, 0:8].unsqueeze(2).to_broadcast([P, 8, 2 * HD]), ALU.mult))
                            pair = tmpA.rearrange("p (s e n) -> p s e n", e=2, n=2 * HD)
                            d = o[:, c, 512:1024].rearrange("p (s n) -> p s n", n=2 * HD)
                            own.link(STT(d, pair[:, :, 1, :], neg_lam[:, 0:1], pair[:, :, 0, :], ALU.mult, ALU.add))
                            own.link(TT(tmpA[:, 0:512].rearrange("p (s n) -> p s n", n=2 * HD), d, d, ALU.mult))
                            own.link(v.tensor_reduce(oss[:, c * 4:c * 4 + 4],
                                                     tmpA[:, 0:512].rearrange("p (s n) -> p s n", n=2 * HD),
                                                     AX_X, ALU.add))
                    else:
                        own.link(v.reciprocal(rinv[:], rsum[:, last - 15:last + 1]))
                        r = rinv[:].rearrange("p (h c) -> p h c", c=2)
                        for c in range(LAT):
                            dst = o[:, c, q["group"] * 512:(q["group"] + 1) * 512].rearrange("p (h n) -> p h n", n=HD)
                            own.link(TT(dst, ps[:, b0 + c, :].rearrange("p (h n) -> p h n", n=HD),
                                        r[:, :, c].unsqueeze(2).to_broadcast([P, 8, HD]), ALU.mult))
                    for b in group_banks(n, q):
                        dve.sem_inc(bank_free[b], 1)

                due = []
                for u in range(len(us)):
                    row_max(u)
                    if due and u == due[0] + 3:
                        group_out(due.pop(0))
                    if us[u]["last"]:
                        due.append(u)
                    if n == 0 and u == A_HEADS:
                        mod_rows_out(1, 0)
                        mod_rows_out(1, 1)
                group_out(due.pop(0))
                dve.sem_inc(keys_free, 1)
                if n == 0:
                    rms(oss[:], ors[:], 2 * HD)
                    for c in range(NCH):
                        d = o[:, c, 512:1024].rearrange("p (s n) -> p s n", n=2 * HD)
                        own.link(TT(d, d, ors[:, 4 * c:4 * c + 4].unsqueeze(2).to_broadcast([P, 4, 2 * HD]), ALU.mult))
                        own.link(TT(d, d, subln[:].unsqueeze(1).to_broadcast([P, 4, 2 * HD]), ALU.mult))
                        dve.sem_inc(on_rdy, 1)
                else:
                    dve.sem_inc(on_rdy, co)
                mod_gain(mod01_in[n][1])
                dve.wait_ge(mod2_in[n][0], 32)
                for t in range(2):
                    for c in range(co):
                        s = 0 if c < LAT else 1
                        cols = slice(t * 512, t * 512 + 512)
                        if t == 1 and c:
                            norm_root(c - 1, c)
                            norm_rows(c - 1, c)
                        take(dve, op_rdy)
                        own.link(TT(ps[:, c, :], ps[:, c, :], mb[:, s, 2, cols], ALU.mult))
                        own.link(TT(xs[:, c, cols], xs[:, c, cols], ps[:, c, :], ALU.add))
                        dve.sem_inc(bank_free[c], 1)
                        if t == 1:
                            dve.sem_inc(x_rdy, 1)
                dve.sem_inc(mod2_free, 1)
                norm_root(co - 1, co)
                norm_rows(co - 1, co)
                if n == 0:
                    mod_rows_out(1, 2)

                def topk16(values, masked, vals, idx):
                    own.link(v.max(vals[:, 0:8], values))
                    own.add(v.max_index(idx[:, 0:8], vals[:, 0:8], values))
                    own.link(v.match_replace(masked, vals[:, 0:8], values, LOWEST))
                    own.link(v.max(vals[:, 8:16], masked))
                    own.link(v.max_index(idx[:, 8:16], vals[:, 8:16], masked))

                def select(col, b):
                    own.link(v.tensor_copy(work.rearrange("p s n -> p (s n)"), scores[:, bass.ds(col, 256)]))
                    for s in range(2):
                        topk16(work[:, s, :], work2[:, s, :], top[:, s, :], topi[:, s, :])
                    own.add(v.tensor_copy(topif[:], topi[:]))
                    c3 = cand.rearrange("p (i j) -> p i j", j=TOPK)
                    own.link(TT(c3, top[:, 0, :].unsqueeze(2).to_broadcast([P, TOPK, TOPK]),
                                top[:, 1, :].unsqueeze(1).to_broadcast([P, TOPK, TOPK]), ALU.add))
                    topk16(cand, cand2, best[:, b, :], bpos[:])
                    own.link(TS(nbest[:, b:b + 1], best[:, b, 0:1], -1.0, None, ALU.mult))
                    dve.sem_inc(best_rdy, 1)
                    own.add(TS(bij[:, 0, :], bpos[:], 4, None, ALU.logical_shift_right))
                    own.link(TS(bij[:, 1, :], bpos[:], TOPK - 1, None, ALU.bitwise_and))
                    own.link(v.tensor_copy(bijf[:], bij[:]))
                    hot = onehot.rearrange("p (s k j) -> p s k j", s=2, k=TOPK)
                    own.link(TT(hot, iota[:].unsqueeze(1).unsqueeze(1).to_broadcast([P, 2, TOPK, TOPK]),
                                bijf[:].unsqueeze(3).to_broadcast([P, 2, TOPK, TOPK]), ALU.is_equal))
                    own.link(TT(hot, hot, topif[:].unsqueeze(2).to_broadcast([P, 2, TOPK, TOPK]), ALU.mult))
                    own.link(v.tensor_reduce(seli[:].rearrange("p s k -> p (s k)"),
                                             onehot.rearrange("p (r j) -> p r j", j=TOPK), AX_X, ALU.add))
                    own.link(STT(expf[:, b, :], seli[:, 0, :], float(NKEYS), seli[:, 1, :], ALU.mult, ALU.add))
                    own.link(v.tensor_copy(idxu[:, b, :], expf[:, b, :]))
                    dve.sem_inc(idxu_rdy, 1)

                def step(g, u_from=0, select_col=None, c_u=None, c_v=None):
                    if g >= LAG - 1:
                        b = (g + 1 - LAG) % TURN
                        v.tensor_copy(idxv[:, b, :], expf[:, b, :]).then_inc(idxv_rdy, 1)
                    if select_col is not None:
                        select(select_col, (g + 1) % TURN)
                    if c_u is not None:
                        b = g % TURN
                        hrow = h[:].rearrange("p c n -> p (c n)")[:, bass.ds(c_u * D, D)]
                        for k in range(TOPK):
                            s = row_slot(g, k)
                            dve.wait_ge(u_in[s], u_from + 16 * rows_landed(n, g, k))
                            own.add(STT(uring[s], uring[s], 1.0, hrow, ALU.mult, ALU.mult,
                                        accum_out=dots[:, b, k:k + 1]))
                            if k:
                                dve.wait_ge(own_v, own.n - 1)
                                dve.sem_inc(u_free, 1)
                        own.wait()
                        dve.sem_inc(u_free, 1)
                        x = dots[:, b, :]
                        own.link(TT(gz[:], x, x, ALU.mult))
                        own.link(TS(gz[:], gz[:], 0.044715, 1.0, ALU.mult, ALU.add))
                        own.link(TT(gz[:], gz[:], x, ALU.mult))
                        dve.sem_inc(gz_rdy, 1)
                        take(dve, gexp_rdy)
                        own.link(v.reciprocal(ginv[:], gsum[:, b:b + 1]))
                        own.link(TT(gz2[:], x, gexp[:, b, :], ALU.mult))
                        own.link(TS(gz2[:], gz2[:], ginv[:, 0:1], 0.5, ALU.mult, ALU.mult))
                        take(dve, gth_rdy)
                        own.link(STT(coef[:, b, :], gth[:], 1.0, gz2[:], ALU.add, ALU.mult))
                        dve.sem_inc(coef_rdy, 1)
                    if c_v is not None:
                        take(dve, y_rdy)
                        yrow = y.rearrange("p c n -> p (c n)")[:, bass.ds(c_v * D, D)]
                        own.link(TT(yrow, ps[:, 0:2, :].rearrange("p b n -> p (b n)"), yrow, ALU.add))
                        for b in range(2):
                            dve.sem_inc(bank_free[b], 1)
                    own.reset()

                if n == 0:
                    dve.wait_ge(mod_out[1], 32 * PARTS)
                    dve.wait_ge(skew_out, 16)
                G = groups[n]
                own.link(v.memset(y[:, 0:co, :], 0.0))
                take(dve, score_rdy)
                dve.sem_inc(peer_go, 1)
                select(0, 0)
                own.reset()
                for g in range(TURN):
                    if g == TURN - 1:
                        take(dve, score_rdy)
                    step(g, 0, (g + 1) * 256, g // 2 % co, None if g < LAG else (g - LAG) // 2 % co)
                take(dve, score_rdy, 2)
                with dve.Fori(0, G // TURN - 2) as i:
                    for j in range(TURN):
                        g = TURN + j
                        step(g, i * (16 * TOPK // RING * TURN), i * (256 * TURN) + (g + 1) * 256,
                             (i * (TURN // 2) + g // 2) % co, (i * (TURN // 2) + (g - LAG) // 2) % co)
                for g in range(G - TURN, G):
                    step(g, 0, (g + 1) * 256 if g < G - 1 else None, g // 2 % co, (g - LAG) // 2 % co)
                step(G)
                if n == 0:
                    dve.sem_inc(u_rows_done, 1)

                def gated(c):
                    s = 0 if c < LAT else 1
                    own.link(TT(y[:, c, :], y[:, c, :], mb[:, s, 2, :], ALU.mult))
                    own.link(TT(xs[:, c, :], xs[:, c, :], y[:, c, :], ALU.add))
                    if n == 0:
                        dve.sem_inc(x_rdy, 1)

                dve.wait_ge(mod2_in[n][1], 32)
                for c in range(co - 1):
                    gated(c)
                step(-1, c_v=co - 1)
                if n == 0:
                    norm_root(0, NCH - 1)
                    mod_gain(mod01_in[1][0])
                    norm_rows(0, NCH - 1)
                step(-1, c_v=co - 1)
                gated(co - 1)
                dve.sem_inc(layer_done if n == 0 else x_out_rdy, 1)


def kernel(**inputs):
    import numpy as _np
    import concourse.bacc as _bacc
    from concourse import mybir as _mybir
    from concourse.bass_utils import run_bass_kernel_spmd as _run

    arrays = {k: _np.ascontiguousarray(v) for k, v in inputs.items()}
    for name in ("peer_u", "peer_v"):
        both = arrays.pop(name)
        for n in range(LAYERS):
            arrays[f"{name}{n}"] = _np.ascontiguousarray(both[n])
    rpb = arrays.pop("c_rpb")
    arrays["rpb_near"] = _np.ascontiguousarray(rpb[0][:, 4:4 + NEAR, :]).reshape(C_HEADS * NEAR, 31)
    arrays.update(constants())
    nc = _bacc.Bacc("TRN2", target_bir_lowering=False, num_devices=1)
    aps = {k: nc.dram_tensor(f"in_{k}", v.shape, _mybir.dt.from_np(v.dtype), kind="ExternalInput").ap()
           for k, v in arrays.items()}
    out = nc.dram_tensor("out_0", (1, SEQ, D), _mybir.dt.float32, kind="ExternalOutput").ap()
    build(nc, aps, out)
    r = _run(nc, [{f"in_{k}": v for k, v in arrays.items()}], core_ids=[0])
    return r.results[0]["out_0"]
```
